# Optimizing a Trainium2 kernel written in Bass

```python
import math
import jax
import jax.numpy as jnp
from jax import lax
import numpy as np

D_MODEL = 1024
BATCH = 1
SEQ = 256
DEPTH = 1

HEAD_DIM = D_MODEL // 16
N_FOX_HEADS = 8
N_MOBA_HEADS = 8
FOX_WIDTH = N_FOX_HEADS * HEAD_DIM
MOBA_WIDTH = N_MOBA_HEADS * HEAD_DIM
IN_COLS = 3 * FOX_WIDTH + N_FOX_HEADS + 3 * MOBA_WIDTH + 2 * D_MODEL
Q_BLOCK = 128
MOBA_BLOCK = 256
MOBA_TOPK = 3
MOBA_Q_CHUNK = 32
PEER_HEADS = 8
PEER_N_KEYS = 128
PEER_N_EXPERTS = PEER_N_KEYS * PEER_N_KEYS
PEER_TOPK = 16
PEER_QUERY_DIM = 256
PEER_HALF = PEER_QUERY_DIM // 2
PEER_TOKEN_CHUNK = 128
EPS = 1e-6
NEG = -1e30

kernel_name = "hybrid_fox_moba_peer_adaln_block"

def rms_norm(x, g):
    xf = x.astype(jnp.float32)
    y = xf * lax.rsqrt(jnp.mean(xf * xf, axis=-1, keepdims=True) + EPS)
    return (y * g.astype(jnp.float32)).astype(x.dtype)

def fox_attention(q, k, v, log_f):
    B, H, S, d = q.shape
    F = jnp.cumsum(log_f, axis=-1)
    nq = S // Q_BLOCK
    qb = q.reshape(B, H, nq, Q_BLOCK, d).transpose(2, 0, 1, 3, 4)
    Fq = F.reshape(B, H, nq, Q_BLOCK).transpose(2, 0, 1, 3)
    kpos = jnp.arange(S)
    scale = d ** -0.5

    def block(args):
        qi, Fi, i = args
        s = jnp.einsum('bhqd,bhkd->bhqk', qi, k).astype(jnp.float32) * scale
        s = s + Fi[..., None] - F[:, :, None, :]
        qpos = i * Q_BLOCK + jnp.arange(Q_BLOCK)
        s = jnp.where(kpos[None, :] <= qpos[:, None], s, NEG)
        p = jax.nn.softmax(s, axis=-1).astype(v.dtype)
        return jnp.einsum('bhqk,bhkd->bhqd', p, v)

    out = lax.map(block, (qb, Fq, jnp.arange(nq)))
    return out.transpose(1, 2, 0, 3, 4).reshape(B, H, S, d)

def moba_attention(q, k, v, slopes):
    B, H, S, d = q.shape
    nb = -(-S // MOBA_BLOCK)
    s_pad = nb * MOBA_BLOCK
    pad = ((0, 0), (0, 0), (0, s_pad - S), (0, 0))
    qp, kp, vp = jnp.pad(q, pad), jnp.pad(k, pad), jnp.pad(v, pad)
    kb = kp.reshape(B, H, nb, MOBA_BLOCK, d)
    vb = vp.reshape(B, H, nb, MOBA_BLOCK, d)
    k_mean = jnp.mean(kb.astype(jnp.float32), axis=3)
    n_sel = min(MOBA_TOPK, nb - 1)
    C = MOBA_Q_CHUNK
    nc = s_pad // C
    qc = qp.reshape(B, H, nc, C, d).transpose(2, 0, 1, 3, 4)
    scale = d ** -0.5
    offs = jnp.arange(MOBA_BLOCK)
    b_idx = jnp.arange(B)[:, None, None, None]
    h_idx = jnp.arange(H)[None, :, None, None]
    slope4 = slopes.astype(jnp.float32)[None, :, None, None]
    slope5 = slope4[..., None]

    def chunk(args):
        qi, ci = args
        t0 = ci * C
        bt = t0 // MOBA_BLOCK
        qpos = t0 + jnp.arange(C)
        k_own = lax.dynamic_index_in_dim(kb, bt, axis=2, keepdims=False)
        v_own = lax.dynamic_index_in_dim(vb, bt, axis=2, keepdims=False)
        own_pos = bt * MOBA_BLOCK + offs
        dist_own = (qpos[:, None] - own_pos[None, :]).astype(jnp.float32)
        s_own = jnp.einsum('bhqd,bhkd->bhqk', qi, k_own).astype(jnp.float32) * scale - slope4 * dist_own
        s_own = jnp.where(dist_own >= 0, s_own, NEG)
        if n_sel == 0:
            p = jax.nn.softmax(s_own, axis=-1).astype(v.dtype)
            return jnp.einsum('bhqk,bhkd->bhqd', p, v_own)
        gate = jnp.einsum('bhqd,bhnd->bhqn', qi.astype(jnp.float32), k_mean)
        gate = jnp.where(jnp.arange(nb) < bt, gate, NEG)
        _, sel = lax.top_k(gate, n_sel)
        k_g = kb[b_idx, h_idx, sel]
        v_g = vb[b_idx, h_idx, sel]
        sel_pos = sel[..., None] * MOBA_BLOCK + offs
        dist_sel = (qpos[None, None, :, None, None] - sel_pos).astype(jnp.float32)
        s_sel = jnp.einsum('bhqd,bhqnkd->bhqnk', qi, k_g).astype(jnp.float32) * scale - slope5 * dist_sel
        s_sel = jnp.where((sel < bt)[..., None], s_sel, NEG)
        logits = jnp.concatenate([s_sel.reshape(B, H, C, n_sel * MOBA_BLOCK), s_own], axis=-1)
        p = jax.nn.softmax(logits, axis=-1).astype(v.dtype)
        p_sel = p[..., :n_sel * MOBA_BLOCK].reshape(B, H, C, n_sel, MOBA_BLOCK)
        p_own = p[..., n_sel * MOBA_BLOCK:]
        return (jnp.einsum('bhqnk,bhqnkd->bhqd', p_sel, v_g)
                + jnp.einsum('bhqk,bhkd->bhqd', p_own, v_own))

    out = lax.map(chunk, (qc, jnp.arange(nc)))
    return out.transpose(1, 2, 0, 3, 4).reshape(B, H, s_pad, d)[:, :, :S]

def peer_ffn(h, w_q, sub_keys, u_tab, v_tab):
    B, S, D = h.shape
    T = B * S
    ht = h.reshape(T, D)
    q = (ht @ w_q).reshape(T, PEER_HEADS, 2, PEER_HALF)
    sc = jnp.einsum('thpc,hpnc->thpn', q, sub_keys).astype(jnp.float32)
    s1, i1 = lax.top_k(sc[:, :, 0], PEER_TOPK)
    s2, i2 = lax.top_k(sc[:, :, 1], PEER_TOPK)
    cand = (s1[..., :, None] + s2[..., None, :]).reshape(T, PEER_HEADS, PEER_TOPK * PEER_TOPK)
    cand_id = (i1[..., :, None] * PEER_N_KEYS + i2[..., None, :]).reshape(T, PEER_HEADS, PEER_TOPK * PEER_TOPK)
    top_s, pos = lax.top_k(cand, PEER_TOPK)
    eid = jnp.take_along_axis(cand_id, pos, axis=-1)
    g = jax.nn.softmax(top_s, axis=-1).astype(h.dtype)
    nc = T // PEER_TOKEN_CHUNK

    def chunk(args):
        hc, ec, gc = args
        a = jnp.einsum('cd,chkd->chk', hc, u_tab[ec])
        w = gc * jax.nn.gelu(a)
        return jnp.einsum('chk,chkd->cd', w, v_tab[ec])

    y = lax.map(chunk, (ht.reshape(nc, PEER_TOKEN_CHUNK, D),
                        eid.reshape(nc, PEER_TOKEN_CHUNK, PEER_HEADS, PEER_TOPK),
                        g.reshape(nc, PEER_TOKEN_CHUNK, PEER_HEADS, PEER_TOPK)))
    return y.reshape(B, S, D)

def setup_inputs(seed: int = 0) -> dict:
    key = jax.random.key(seed)
    ks = jax.random.split(key, 20)
    D = D_MODEL
    nrm = lambda k, shape, s: jax.random.normal(k, shape, jnp.float32) * s
    return {
        "x": nrm(ks[0], (BATCH, SEQ, D), 1.0),
        "c": nrm(ks[1], (BATCH, D), 1.0),
        "w_ada": nrm(ks[2], (DEPTH, D, 6 * D), D ** -0.5),
        "b_ada": nrm(ks[3], (DEPTH, 6 * D), 0.02),
        "norm1_g": 1.0 + nrm(ks[4], (DEPTH, D), 0.05),
        "w_in": nrm(ks[5], (DEPTH, D, IN_COLS), D ** -0.5),
        "b_fgate": jnp.linspace(1.0, 4.0, N_FOX_HEADS, dtype=jnp.float32)[None, :] + nrm(ks[6], (DEPTH, N_FOX_HEADS), 0.1),
        "fox_q_g": 1.0 + nrm(ks[7], (DEPTH, HEAD_DIM), 0.05),
        "fox_k_g": 1.0 + nrm(ks[8], (DEPTH, HEAD_DIM), 0.05),
        "moba_q_g": 1.0 + nrm(ks[9], (DEPTH, HEAD_DIM), 0.05),
        "moba_k_g": 1.0 + nrm(ks[10], (DEPTH, HEAD_DIM), 0.05),
        "w_up_fox": nrm(ks[11], (DEPTH, FOX_WIDTH, D), FOX_WIDTH ** -0.5),
        "w_up_moba": nrm(ks[12], (DEPTH, MOBA_WIDTH, D), MOBA_WIDTH ** -0.5),
        "w_out": nrm(ks[13], (DEPTH, D, D), D ** -0.5),
        "norm2_g": 1.0 + nrm(ks[14], (DEPTH, D), 0.05),
        "w_peer_q": nrm(ks[15], (DEPTH, D, PEER_HEADS * PEER_QUERY_DIM), D ** -0.5),
        "peer_sub_keys": nrm(ks[16], (DEPTH, PEER_HEADS, 2, PEER_N_KEYS, PEER_HALF), PEER_HALF ** -0.5),
        "peer_u": nrm(ks[17], (DEPTH, PEER_N_EXPERTS, D), D ** -0.5),
        "peer_v": nrm(ks[18], (DEPTH, PEER_N_EXPERTS, D), (PEER_HEADS * PEER_TOPK) ** -0.5),
    }

def reference(x, c, w_ada, b_ada, norm1_g, w_in, b_fgate, fox_q_g, fox_k_g, moba_q_g, moba_k_g,
              w_up_fox, w_up_moba, w_out, norm2_g, w_peer_q, peer_sub_keys, peer_u, peer_v):
    B, S, D = x.shape
    slopes = 2.0 ** (-8.0 * jnp.arange(1, N_MOBA_HEADS + 1, dtype=jnp.float32) / N_MOBA_HEADS)
    split_at = list(np.cumsum([FOX_WIDTH, FOX_WIDTH, FOX_WIDTH, N_FOX_HEADS,
                               MOBA_WIDTH, MOBA_WIDTH, MOBA_WIDTH, D_MODEL]))

    def heads(t, n_h):
        return t.reshape(B, S, n_h, HEAD_DIM).transpose(0, 2, 1, 3)

    def merge_heads(t):
        return t.transpose(0, 2, 1, 3).reshape(B, S, -1)

    silu_c = jax.nn.silu(c)
    for l in range(DEPTH):
        mod = (silu_c @ w_ada[l] + b_ada[l])[:, None, :]
        shift1, scale1, gate1, shift2, scale2, gate2 = jnp.split(mod, 6, axis=-1)

        h = rms_norm(x, norm1_g[l]) * (1.0 + scale1) + shift1
        z = h @ w_in[l]
        q_a, k_a, v_a, f_a, q_b, k_b, v_b, g_a, g_b = jnp.split(z, split_at, axis=-1)

        q_a = rms_norm(heads(q_a, N_FOX_HEADS), fox_q_g[l])
        k_a = rms_norm(heads(k_a, N_FOX_HEADS), fox_k_g[l])
        log_f = jax.nn.log_sigmoid((f_a + b_fgate[l]).astype(jnp.float32)).transpose(0, 2, 1)
        y_a = merge_heads(fox_attention(q_a, k_a, heads(v_a, N_FOX_HEADS), log_f))

        q_b = rms_norm(heads(q_b, N_MOBA_HEADS), moba_q_g[l])
        k_b = rms_norm(heads(k_b, N_MOBA_HEADS), moba_k_g[l])
        y_b = merge_heads(moba_attention(q_b, k_b, heads(v_b, N_MOBA_HEADS), slopes))

        mixed = jax.nn.sigmoid(g_a) * (y_a @ w_up_fox[l]) + jax.nn.sigmoid(g_b) * (y_b @ w_up_moba[l])
        x = x + gate1 * (mixed @ w_out[l])

        h2 = rms_norm(x, norm2_g[l]) * (1.0 + scale2) + shift2
        x = x + gate2 * peer_ffn(h2, w_peer_q[l], peer_sub_keys[l], peer_u[l], peer_v[l])
    return x


_drawn_inputs = setup_inputs


def setup_inputs(seed=0):
    import zlib

    import numpy as np

    out = dict(_drawn_inputs(seed))
    spreads = {}
    factors = {'b_ada': 3.555,
     'norm1_g': 3.81,
     'fox_q_g': 8.0,
     'fox_k_g': 8.0,
     'moba_q_g': 8.0,
     'moba_k_g': 8.0,
     'norm2_g': 7.963}
    for name, (base, spread) in spreads.items():
        noise = np.random.default_rng([zlib.crc32(name.encode()), seed]).standard_normal(out[name].shape)
        drawn = base * np.exp(spread * noise) if base else spread * noise
        out[name] = jnp.asarray(drawn.astype(out[name].dtype))
    for name, factor in factors.items():
        out[name] = (out[name] * factor).astype(out[name].dtype)
    return out
```

```python
from contextlib import ExitStack

import concourse.bass as bass
from concourse import mybir

F32 = mybir.dt.float32
U32 = mybir.dt.uint32
I32 = mybir.dt.int32
ALU = mybir.AluOpType
ACT = mybir.ActivationFunctionType
AX_X = mybir.AxisListType.X

P = 128
EPS = 1e-6
NEG = -1e30
HD = 64
HEADS = 8
TOPK = 16
LISTS = 2 * HEADS
WIDE = 4
NARROW = 4
NCAND = WIDE * TOPK + (TOPK - WIDE) * NARROW
NW = 4
NL = 2
NU = 8
NV = 8
ND = 8
NB = 6
NS = 4
QA, KA, VA, QB, KB, VB = range(6)
NZ = 10
ADA = 12
ADA_FIRST = 4


def psum_plan(tiles):
    items = ["cols"] + [("ada", n) for n in range(ADA_FIRST)]
    items += [("xT", t, h) for t in range(tiles) for h in range(2)]
    items += z_order(tiles)
    items += [("ada", n) for n in range(ADA_FIRST, ADA)] + [("row", r, h) for r in range(4) for h in range(2)]
    items += [("skT", n) for n in range(4)]
    for t in range(tiles):
        for g in range(2):
            for s in range(HEADS + 3):
                if s < HEADS:
                    items.append(("S", t, g, s))
                if 0 <= s - 2 < HEADS:
                    items.append(("PT", t, g, s - 2))
                if 0 <= s - 3 < HEADS and (s - 3) % 2 == 1:
                    items.append(("y", t, g, (s - 3) // 2))
        for c in range(2):
            items += [("up", t, c, g) for g in range(2)]
        items += [("mixT", t, h) for h in range(2)]
        items += [("o", t, q) for q in range(4)]
        items += [("h2T", t, h) for h in range(2)]
        for n in range(LISTS // 4):
            items += [("qp", t, 2 * n), ("qp", t, 2 * n + 1), ("sc", t, n)]
    return {key: n for n, key in enumerate(items)}


def z_order(tiles):
    items = ["f"]
    late = []
    for c in range(NZ):
        items += [("z", c, t) for t in range(tiles)]
        items += late
        late = [("qkT", c, t) for t in range(tiles)] if c in (QA, KA, QB, KB) else []
        if c == VA:
            items.append("Fcol")
    return items + late


def block_kernel(nc, x, c, w_ada, b_ada, norm1_g, w_in, b_fgate, fox_q_g, fox_k_g, moba_q_g, moba_k_g,
                 w_up_fox, w_up_moba, w_out, norm2_g, w_peer_q, peer_sub_keys, peer_u, peer_v, out):
    T, D = x.shape[1], x.shape[2]
    TILES = T // P
    KD = D // P
    HALF = D // 2
    NG = TILES * HEADS
    GW = HEADS * HD
    F_AT = 3 * GW
    z_at = [0, GW, 2 * GW] + [F_AT + HEADS + n * GW for n in range(NZ - 3)]
    slopes = [2.0 ** (-8.0 * (h + 1) / HEADS) for h in range(HEADS)]
    plan = psum_plan(TILES)
    assert TILES == 2 and KD == 8 and GW == 512

    chunks = [("ada", n) for n in range(ADA_FIRST)] + [("z", n) for n in range(NZ)]
    chunks += [("ada", n) for n in range(ADA_FIRST, ADA)] + [("sk", 0)]
    chunk_no = {key: n for n, key in enumerate(chunks)}
    late = [("up", c, g) for c in range(2) for g in range(2)]
    late += [("out", n) for n in range(4)] + [("peer", n) for n in range(8)]
    late_no = {key: n for n, key in enumerate(late)}

    with ExitStack() as ctx:
        def sb(name, shape, dt=F32):
            return ctx.enter_context(nc.sbuf_tensor(name, shape, dt))

        def sem(name):
            return ctx.enter_context(nc.semaphore(name))

        ring = sb("ring", [P, NW, KD, 512])
        uv = ring[:].rearrange("p a k n -> p (a k n)").rearrange("p (s d) -> p s d", d=D)
        ubuf, vbuf = uv[:, 0:NU, :], uv[:, NU:NU + NV, :]
        late_ring = sb("late_ring", [P, NL, 2048])
        x_sb = sb("x_sb", [P, TILES, D])
        hT = sb("hT", [P, KD, T])
        sc = hT[:].rearrange("p k t -> p (k t)")
        tT = sb("tT", [P, KD, P])
        qkT = sb("qkT", [P, 4, 4, T])
        v_sb = sb("v_sb", [P, TILES, 2, GW])
        gates = sb("gates", [P, TILES, 4, 512])
        h2 = gates[:, 0, :, :].rearrange("p a n -> p (a n)").rearrange("p (t d) -> p t d", t=TILES)
        rows = sb("rows", [P, 4, D])
        skT = sb("skT", [P, LISTS, P])
        diag = sb("diag", [P, ND, P])
        score = sb("score", [P, NS, T])
        pT = sb("pT", [P, 2, TILES, P])
        tmp = sb("tmp", [P, 2, 512])
        qn = score[:].rearrange("p a n -> p (a n)").rearrange("p (a n) -> p a n", n=512)
        cand = score[:].rearrange("p a n -> p (a n)")[:, 0:HEADS * NCAND].rearrange("p (h n) -> p h n", h=HEADS)
        wide = sb("wide", [P, D])
        yT = sb("yT", [P, 2, 4, P])
        spare = yT[:].rearrange("p a b n -> p (a b n)")
        dist_i = spare[:, 0:T].bitcast(I32)
        pw = spare[:, 0:512].bitcast(U32).rearrange("p (a n) -> p a n", a=4)
        pf = spare[:, 512:1024].rearrange("p (a n) -> p a n", a=4)
        i16f = pT[:].rearrange("p a b n -> p (a b n)")[:, 0:LISTS * TOPK].rearrange("p (l k) -> p l k", k=TOPK)
        qp = sb("qp", [P, 2, 2, P])
        raw = sb("raw", [76, P])
        cols = sb("cols", [P, 76])
        silu = sb("silu", [P, KD])
        mod = sb("mod", [P, 48])
        a1 = sb("a1", [P, KD])
        a2 = sb("a2", [P, KD])
        wf = sb("wf", [P, KD, HEADS])
        bf = sb("bf", [HEADS, 1])
        fx = sb("fx", [HEADS, 4, T])
        sel = sb("sel", [HEADS, HEADS, P])
        fcol = sb("fcol", [P, TILES, HEADS])
        ident = sb("ident", [P, P])
        ones = sb("ones", [P, P])
        mask = sb("mask", [P, T])
        dist = sb("dist", [P, T])
        iota_i = sb("iota_i", [P, TOPK], I32)
        iota_f = sb("iota_f", [P, TOPK])
        ss = sb("ss", [P, HEADS])
        nrm = sb("nrm", [P, 4, HEADS])
        mx = sb("mx", [P, 2, HEADS])
        rsum = sb("rsum", [P, 2, HEADS])
        v16 = sb("v16", [P, LISTS, TOPK])
        i16 = sb("i16", [P, LISTS, TOPK], U32)
        tv = sb("tv", [P, HEADS, TOPK])
        pos = sb("pos", [P, HEADS * TOPK], U32)
        gsum = sb("gsum", [P, 2, HEADS])
        g_sb = sb("g_sb", [P, NG * TOPK])
        eid = sb("eid", [P, NG * TOPK], I32)
        idx = sb("idx", [P, 3, TOPK], I32)
        adot = sb("adot", [P, 2, TOPK])
        gel = sb("gel", [P, TOPK])
        ew = sb("ew", [P, 2, TOPK])

        banks = [ctx.enter_context(nc.psum_tensor(f"bank{b}", [P, 512], F32)) for b in range(NB)]
        ps_y = ctx.enter_context(nc.psum_tensor("ps_y", [P, D], F32))

        s_small = sem("small_loaded")
        s_x = sem("x_loaded")
        s_chunk = [sem(f"chunk_landed{n}") for n in range(NW)]
        s_late = [sem(f"late_landed{n}") for n in range(NL)]
        s_const = sem("constants_ready")
        s_pool = sem("pool_step")
        s_dve = sem("dve_step")
        s_item = sem("psum_item_ready")
        s_bank = [sem(f"bank_read{b}") for b in range(NB)]
        s_sig = sem("sigmoid_c_ready")
        s_silu = sem("silu_ready")
        s_sq = sem("squares_ready")
        s_var = sem("variance_ready")
        s_root = sem("root_ready")
        s_xn = sem("row_ready_for_transpose")
        s_fneg = sem("minus_abs_f_ready")
        s_fexp = sem("exp_f_ready")
        s_fone = sem("one_plus_exp_ready")
        s_fln = sem("log_ready")
        s_F = sem("F_ready")
        s_mod = sem("modulation_ready")
        s_dg = sem("column_diagonal_ready")
        s_sc_max = sem("score_max_ready")
        s_exp = sem("exp_ready")
        s_prob = sem("prob_ready")
        s_x1 = sem("x1_ready")
        s_g0 = sem("top_scores_shifted")
        s_g1 = sem("top_scores_exp")
        s_eid = sem("expert_ids_ready")
        s_idx = sem("idx_ready")
        s_free = sem("row_slot_seen_free")
        s_u = [sem(f"u_landed{n}") for n in range(NU)]
        s_v = [sem(f"v_landed{n}") for n in range(NV)]
        s_ufree = sem("u_slots_free")
        s_vfree = sem("v_slots_free")
        s_gelu = sem("gelu_ready")
        s_ew = sem("expert_weights_ready")
        s_diag = sem("diag_ready")
        s_ytaken = sem("y_read")
        s_yrow = sem("y_row_ready")
        s_stored = sem("stored")

        def bank(key):
            return banks[plan[key] % NB]

        def await_item(eng, key):
            eng.wait_ge(s_item, plan[key] + 1)

        def read(ins, key):
            return ins.then_inc(s_bank[plan[key] % NB], 1)

        def await_read(eng, key):
            eng.wait_ge(s_bank[plan[key] % NB], plan[key] // NB + 1)

        def chunk_user(n):
            what, m = chunks[n]
            return {"ada": ("ada", m), "z": ("z", m, TILES - 1), "sk": ("skT", 3)}[what]

        def late_user(no):
            t, what = no // len(late), late[no % len(late)]
            return {"up": ("up", t) + what[1:], "out": ("o", t) + what[1:], "peer": ("qp", t) + what[1:]}[what[0]]

        block = ctx.enter_context(nc.Block())

        @block.sync
        def _(sp):
            def late_chunk(t, n):
                no = t * len(late) + n
                if no >= NL:
                    await_item(sp, late_user(no - NL))
                what = late[n]
                dst = late_ring[:, no % NL, :]
                if what[0] == "up":
                    src = (w_up_fox, w_up_moba)[what[2]][0].rearrange("(k p) n -> p k n", p=P)
                    src = src[:, :, what[1] * 512:(what[1] + 1) * 512]
                    dst = dst.rearrange("p (k n) -> p k n", n=512)
                else:
                    src = (w_out if what[0] == "out" else w_peer_q)[0].rearrange("(k p) n -> p k n", p=P)
                    src = src[:, :, what[1] * 256:(what[1] + 1) * 256]
                    dst = dst.rearrange("p (k n) -> p k n", n=256)
                sp.dma_start(dst, src).then_inc(s_late[no % NL], 16)

            sp.dma_start(x_sb[:], x[0].rearrange("(t p) d -> p t d", p=P)).then_inc(s_x, 16)
            for n, (what, m) in enumerate(chunks):
                if n >= NW:
                    await_item(sp, chunk_user(n - NW))
                dst = ring[:, n % NW, :, :]
                if what == "sk":
                    src = peer_sub_keys[0].rearrange("h q n c -> n (h q) c")
                    dst = dst[:, 0:4, :].rearrange("p k (l c) -> p (k l) c", c=P)
                else:
                    w = (w_ada if what == "ada" else w_in)[0].rearrange("(k p) n -> p k n", p=P)
                    at = m * 512 if what == "ada" else z_at[m]
                    src = w[:, :, at:at + 512]
                sp.dma_start(dst, src).then_inc(s_chunk[n % NW], 16)
            for t in range(TILES):
                for n in range(len(late)):
                    late_chunk(t, n)
            for t in range(TILES):
                sp.wait_ge(s_yrow, t + 1)
                sp.dma_start(out[0, t * P:(t + 1) * P, :], wide[:]).then_inc(s_stored, 16)
            sp.wait_ge(s_stored, 16 * TILES)

        @block.gpsimd
        def _(pool):
            pool.memset(ones[:], 1.0).then_inc(s_pool, 1)
            pool.memset(ident[:], 0.0).then_inc(s_pool, 1)
            pool.memset(mask[:], 0.0).then_inc(s_pool, 1)
            pool.memset(sel[:], 0.0).then_inc(s_pool, 1)
            pool.iota(dist_i, pattern=[[-1, T]], base=P, channel_multiplier=1).then_inc(s_pool, 1)
            pool.iota(iota_i[:], pattern=[[1, TOPK]], base=0, channel_multiplier=0).then_inc(s_pool, 1)
            pool.wait_ge(s_pool, 6)
            pool.affine_select(out=ident[:], in_=ident[:], compare_op=ALU.not_equal, fill=1.0, base=0,
                               pattern=[[-1, P]], channel_multiplier=1).then_inc(s_const, 1)
            pool.affine_select(out=mask[:], in_=mask[:], compare_op=ALU.is_ge, fill=NEG, base=P,
                               pattern=[[-1, T]], channel_multiplier=1).then_inc(s_const, 1)
            pool.affine_select(out=sel[:], in_=sel[:], compare_op=ALU.not_equal, fill=1.0, base=0,
                               pattern=[[-1, HEADS], [0, P]], channel_multiplier=1).then_inc(s_const, 1)
            pool.tensor_copy(dist[:], dist_i).then_inc(s_pool, 1)
            pool.tensor_copy(iota_f[:], iota_i[:]).then_inc(s_const, 1)
            pool.wait_ge(s_pool, 7)
            pool.affine_select(out=dist[:], in_=dist[:], compare_op=ALU.is_ge, fill=-NEG, base=P,
                               pattern=[[-1, T]], channel_multiplier=1).then_inc(s_const, 1)

            pool.sem_inc(s_ufree, NU)
            pool.sem_inc(s_vfree, NV)

            def take(i, r):
                pool.wait_ge(s_eid, i + 1)
                pool.sem_inc(s_free, 1)
                pool.tensor_copy(idx[:, r, :], eid[:, bass.ds(i * TOPK, TOPK)]).then_inc(s_idx, 1)
                pool.wait_ge(s_idx, i + 1)
                pool.sem_inc(s_free, 1)

            def fetch_u(i, k, r):
                pool.wait_ge(s_ufree, i * TOPK + k + 1)
                pool.sem_inc(s_free, 1)
                pool.indirect_dma_start(
                    ubuf[:, k % NU, :], None, peer_u[0],
                    bass.IndirectOffsetOnAxis(ap=idx[:, r, k:k + 1], axis=0)).then_inc(s_u[k % NU], 16)

            def fetch_v(i, k, r):
                pool.wait_ge(s_vfree, i * TOPK + k + 1)
                pool.sem_inc(s_free, 1)
                pool.indirect_dma_start(
                    vbuf[:, k % NV, :], None, peer_v[0],
                    bass.IndirectOffsetOnAxis(ap=idx[:, r, k:k + 1], axis=0)).then_inc(s_v[k % NV], 16)

            take(0, 0)
            for k in range(TOPK):
                fetch_u(0, k, 0)
            with pool.Fori(0, (NG - 1) // 3) as n:
                for j in range(3):
                    i = n * 3 + (1 + j)
                    take(i, (j + 1) % 3)
                    for k in range(TOPK):
                        fetch_u(i, k, (j + 1) % 3)
                        fetch_v(i - 1, k, j)
            for k in range(TOPK):
                fetch_v(NG - 1, k, 0)

        @block.vector
        def _(dve):
            steps = [0]

            def link(ins):
                steps[0] += 1
                ins.then_inc(s_dve, 1)
                dve.wait_ge(s_dve, steps[0])

            roots = [0]
            squares = [0]

            def inverse_root(n, count):
                v, r, q, m = (nrm[:, j, 0:count] for j in range(4))
                roots[0] += 1
                dve.tensor_scalar(v, ss[:, 0:count], 1.0 / n, EPS, ALU.mult, ALU.add).then_inc(s_var, 1)
                dve.wait_ge(s_root, roots[0])
                link(dve.reciprocal(r, q))
                link(dve.tensor_tensor(m, r, r, ALU.mult))
                link(dve.tensor_tensor(m, m, v, ALU.mult))
                link(dve.tensor_scalar(m, m, -0.5, 1.5, ALU.mult, ALU.add))
                link(dve.tensor_tensor(v, r, m, ALU.mult))

            def modulation(first, last):
                for n in range(first, last):
                    key = ("ada", n)
                    await_item(dve, key)
                    read(dve.tensor_tensor(mod[:, 4 * n:4 * n + 4], bank(key)[:, 0:4],
                                           cols[:, 24 + 4 * n:28 + 4 * n], ALU.add), key)
                await_read(dve, ("ada", last - 1))

            await_item(dve, "cols")
            read(dve.tensor_copy(cols[:], bank("cols")[:, 0:76]), "cols")
            await_read(dve, "cols")
            link(dve.tensor_scalar(cols[:, 72:73], cols[:, 72:73], HD ** -0.5, None, ALU.mult))
            link(dve.tensor_scalar(cols[:, 74:75], cols[:, 74:75], HD ** -0.5, None, ALU.mult))
            dve.wait_ge(s_sig, 1)
            dve.tensor_tensor(silu[:], silu[:], cols[:, 0:KD], ALU.mult).then_inc(s_silu, 1)

            for t in range(TILES):
                dve.wait_ge(s_sq, t + 1)
                inverse_root(D, 1)
                if t:
                    await_item(dve, ("xT", t - 1, 1))
                dve.tensor_scalar(wide[:], x_sb[:, t, :], nrm[:, 0, 0:1], None, ALU.mult).then_inc(s_xn, 1)
                dve.wait_ge(s_xn, t + 1)
                if t == 0:
                    modulation(0, ADA_FIRST)
                    link(dve.scalar_tensor_tensor(out=a1[:], in0=mod[:, 8:16], scalar=1.0, in1=cols[:, 8:16],
                                                  op0=ALU.add, op1=ALU.mult))
                for h in range(2):
                    key = ("xT", t, h)
                    await_item(dve, key)
                    for j in range(4):
                        k = 4 * h + j
                        ins = dve.tensor_scalar(hT[:, k, t * P:(t + 1) * P], bank(key)[:, j * P:(j + 1) * P],
                                                a1[:, k:k + 1], mod[:, k:k + 1], ALU.mult, ALU.add)
                    read(ins, key)

            def forget_gates():
                xs, a, b, neg = (fx[:, n, :] for n in range(4))
                await_item(dve, "f")
                dve.wait_ge(s_small, 14 * 16)
                read(dve.tensor_scalar(xs, bank("f")[0:HEADS, 0:T], bf[:, 0:1], None, ALU.add), "f")
                await_read(dve, "f")
                link(dve.scalar_tensor_tensor(out=a, in0=xs, scalar=-1.0, in1=xs, op0=ALU.mult, op1=ALU.min))
                dve.tensor_scalar(xs, xs, 0.0, None, ALU.min).then_inc(s_fneg, 1)
                dve.wait_ge(s_fneg, 1)
                dve.wait_ge(s_fexp, 1)
                dve.tensor_scalar(b, b, 1.0, None, ALU.add).then_inc(s_fone, 1)
                dve.wait_ge(s_fln, 1)
                link(dve.tensor_tensor(xs, xs, a, ALU.subtract))
                link(dve.memset(b, 1.0))
                link(dve.tensor_tensor_scan(a, b, xs, 0.0, ALU.mult, ALU.add))
                dve.tensor_scalar(neg, a, -1.0, None, ALU.mult).then_inc(s_F, 1)

            forget_gates()
            norms = 0
            for c_ in range(NZ):
                if c_ == QB:
                    await_item(dve, "Fcol")
                    dve.tensor_copy(fcol[:].rearrange("p t h -> p (t h)"),
                                    bank("Fcol")[:, 0:TILES * HEADS]).then_inc(s_bank[plan["Fcol"] % NB], 1)
                if c_ not in (QA, KA, QB, KB):
                    continue
                for t in range(TILES):
                    key = ("z", c_, t)
                    dve.wait_ge(s_sq, TILES + norms + 1)
                    link(dve.tensor_reduce(ss[:], tmp[:, norms % 2, :].rearrange("p (h d) -> p h d", d=HD),
                                           AX_X, ALU.add))
                    inverse_root(HD, HEADS)
                    if norms >= 2:
                        pc, pt = [(a, b) for a in (QA, KA, QB, KB) for b in range(TILES)][norms - 2]
                        await_item(dve, ("qkT", pc, pt))
                    ins = dve.tensor_tensor(
                        qn[:, norms % 2, :].rearrange("p (h d) -> p h d", d=HD),
                        bank(key)[:].rearrange("p (h d) -> p h d", d=HD),
                        nrm[:, 0, :].unsqueeze(2).to_broadcast([P, HEADS, HD]), ALU.mult)
                    read(ins, key)
                    norms += 1
            modulation(ADA_FIRST, ADA)
            dve.scalar_tensor_tensor(out=a2[:], in0=mod[:, 32:40], scalar=1.0, in1=cols[:, 16:24],
                                     op0=ALU.add, op1=ALU.mult).then_inc(s_mod, 1)
            for r in range(4):
                for h in range(2):
                    key = ("row", r, h)
                    await_item(dve, key)
                    read(dve.tensor_copy(rows[:, r, h * HALF:(h + 1) * HALF], bank(key)[:]), key)

            def attention(t, g):
                nk = (t + 1) * P
                n0 = (t * 2 + g) * HEADS
                par = g
                for s in range(HEADS + 1):
                    if s < HEADS:
                        key = ("S", t, g, s)
                        sl = score[:, s % NS, 0:nk]
                        await_item(dve, key)
                        if n0 + s >= NS:
                            o = n0 + s - NS
                            await_item(dve, ("PT", o // (2 * HEADS), o // HEADS % 2, o % HEADS))
                        if g == 0:
                            ins = dve.scalar_tensor_tensor(out=sl, in0=bank(key)[:, 0:nk], scalar=fcol[:, t, s:s + 1],
                                                           in1=mask[:, T - nk:T], op0=ALU.add, op1=ALU.add)
                        else:
                            ins = dve.scalar_tensor_tensor(out=sl, in0=dist[:, T - nk:T], scalar=-slopes[s],
                                                           in1=bank(key)[:, 0:nk], op0=ALU.mult, op1=ALU.add)
                        read(ins, key)
                        await_read(dve, key)
                        link(dve.tensor_reduce(mx[:, par, s:s + 1], sl, AX_X, ALU.max))
                        dve.tensor_scalar(mx[:, par, s:s + 1], mx[:, par, s:s + 1], -1.0, None,
                                          ALU.mult).then_inc(s_sc_max, 1)
                    if s >= 1:
                        o = s - 1
                        dve.wait_ge(s_exp, n0 + o + 1)
                        link(dve.reciprocal(rsum[:, par, o:o + 1], rsum[:, par, o:o + 1]))
                        po = score[:, o % NS, 0:nk]
                        dve.tensor_scalar(po, po, rsum[:, par, o:o + 1], None, ALU.mult).then_inc(s_prob, 1)

            def up(t):
                for c_ in range(2):
                    for g in range(2):
                        key = ("up", t, c_, g)
                        await_item(dve, key)
                        if t == 0 and c_ == 0 and g == 0:
                            for u in range(TILES):
                                for m in range(6, NZ):
                                    await_read(dve, ("z", m, u))
                        read(dve.tensor_tensor(tmp[:, g, :], gates[:, t, 2 * g + c_, :], bank(key)[:], ALU.mult), key)
                        await_read(dve, key)
                    dve.tensor_tensor(wide[:, c_ * 512:(c_ + 1) * 512], tmp[:, 0, :], tmp[:, 1, :],
                                      ALU.add).then_inc(s_xn, 1)
                    dve.wait_ge(s_xn, TILES + t * 3 + c_ + 1)

            def out_part(t):
                for q in range(4):
                    key = ("o", t, q)
                    cut = slice(q * 256, (q + 1) * 256)
                    await_item(dve, key)
                    read(dve.tensor_tensor(tmp[:, q % 2, 0:256], bank(key)[:, 0:256], rows[:, 0, cut], ALU.mult), key)
                    await_read(dve, key)
                    dve.tensor_tensor(x_sb[:, t, cut], x_sb[:, t, cut], tmp[:, q % 2, 0:256],
                                      ALU.add).then_inc(s_x1, 1)
                    dve.wait_ge(s_x1, t * 4 + q + 1)
                dve.wait_ge(s_sq, TILES + 4 * TILES + t + 1)
                inverse_root(D, 1)
                link(dve.scalar_tensor_tensor(out=h2[:, t, :], in0=x_sb[:, t, :], scalar=nrm[:, 0, 0:1],
                                              in1=rows[:, 1, :], op0=ALU.mult, op1=ALU.mult))
                dve.tensor_tensor(h2[:, t, :], h2[:, t, :], rows[:, 2, :], ALU.add).then_inc(s_xn, 1)
                dve.wait_ge(s_xn, TILES + t * 3 + 3)

            def top16(values, indices, scores, n):
                for half in range(2):
                    cut = slice(8 * half, 8 * half + 8)
                    for l in range(n):
                        ins = dve.max(values(l)[:, cut], scores(l))
                    link(ins)
                    for l in range(n):
                        ins = dve.max_index(indices(l)[:, cut], values(l)[:, cut], scores(l))
                    link(ins)
                    if half == 0:
                        for l in range(n):
                            ins = dve.match_replace(scores(l), values(l)[:, cut], scores(l), -3.0e38)
                        link(ins)

            def choose_keys(t, part):
                for n in (2 * part, 2 * part + 1):
                    await_read(dve, ("sc", t, n))
                top16(lambda l: v16[:, part * 8 + l, :], lambda l: i16[:, part * 8 + l, :],
                      lambda l: sc[:, (part * 8 + l) * P:(part * 8 + l + 1) * P], 8)

            def choose_experts(t):
                s1 = v16[:].rearrange("p (h q) k -> p h q k", q=2)
                link(dve.tensor_copy(i16f, i16[:]))
                c1 = cand[:, :, 0:WIDE * TOPK].rearrange("p h (a b) -> p h a b", b=TOPK)
                c2 = cand[:, :, WIDE * TOPK:NCAND].rearrange("p h (a b) -> p h a b", b=NARROW)
                link(dve.tensor_tensor(c1, s1[:, :, 0, 0:WIDE].unsqueeze(3).to_broadcast([P, HEADS, WIDE, TOPK]),
                                       s1[:, :, 1, :].unsqueeze(2).to_broadcast([P, HEADS, WIDE, TOPK]), ALU.add))
                link(dve.tensor_tensor(
                    c2, s1[:, :, 0, WIDE:TOPK].unsqueeze(3).to_broadcast([P, HEADS, TOPK - WIDE, NARROW]),
                    s1[:, :, 1, 0:NARROW].unsqueeze(2).to_broadcast([P, HEADS, TOPK - WIDE, NARROW]), ALU.add))
                p3 = pos[:].rearrange("p (h k) -> p h k", k=TOPK)
                top16(lambda l: tv[:, l, :], lambda l: p3[:, l, :], lambda l: cand[:, l, :], HEADS)
                gt = g_sb[:, t * P:(t + 1) * P].rearrange("p (h k) -> p h k", k=TOPK)
                dve.tensor_tensor(gt, tv[:], tv[:, :, 0:1].to_broadcast([P, HEADS, TOPK]),
                                  ALU.subtract).then_inc(s_g0, 1)
                lo, hi, l2, h2_ = (pw[:, n, :] for n in range(4))
                af, bf_, m, d = (pf[:, n, :] for n in range(4))
                link(dve.tensor_scalar(hi, pos[:], 4, None, ALU.logical_shift_right))
                link(dve.tensor_scalar(lo, pos[:], TOPK - 1, None, ALU.bitwise_and))
                link(dve.tensor_scalar(h2_, pos[:], 2, None, ALU.logical_shift_right))
                link(dve.tensor_scalar(l2, pos[:], NARROW - 1, None, ALU.bitwise_and))
                link(dve.tensor_scalar(m, pos[:], float(WIDE * TOPK), None, ALU.is_ge))
                link(dve.scalar_tensor_tensor(out=d, in0=h2_, scalar=float(WIDE - WIDE * TOPK // NARROW), in1=hi,
                                              op0=ALU.add, op1=ALU.subtract))
                link(dve.tensor_tensor(d, d, m, ALU.mult))
                link(dve.tensor_tensor(af, d, hi, ALU.add))
                link(dve.tensor_tensor(d, l2, lo, ALU.subtract))
                link(dve.tensor_tensor(d, d, m, ALU.mult))
                link(dve.tensor_tensor(bf_, d, lo, ALU.add))
                ii = i16f.rearrange("p (h q) k -> p h q k", q=2)
                oh = sc.rearrange("p (h k r) -> p h k r", h=HEADS, k=TOPK)
                oh2 = sc.rearrange("p (k r) -> p k r", r=TOPK)
                for rank, q, to in ((af, 0, m), (bf_, 1, d)):
                    link(dve.tensor_tensor(oh2, rank.unsqueeze(2).to_broadcast([P, P, TOPK]),
                                           iota_f[:].unsqueeze(1).to_broadcast([P, P, TOPK]), ALU.is_equal))
                    link(dve.tensor_tensor(oh, oh, ii[:, :, q, :].unsqueeze(2).to_broadcast([P, HEADS, TOPK, TOPK]),
                                           ALU.mult))
                    link(dve.tensor_reduce(to, oh2, AX_X, ALU.add))
                dve.scalar_tensor_tensor(out=eid[:, t * P:(t + 1) * P], in0=m, scalar=float(P), in1=d,
                                         op0=ALU.mult, op1=ALU.add).then_inc(s_eid, HEADS)
                dve.wait_ge(s_g1, t + 1)
                link(dve.tensor_reduce(gsum[:, 0, :], gt, AX_X, ALU.add))
                link(dve.reciprocal(gsum[:, 1, :], gsum[:, 0, :]))
                link(dve.tensor_tensor(gt, gt, gsum[:, 1, :].unsqueeze(2).to_broadcast([P, HEADS, TOPK]), ALU.mult))

            stages = [lambda t: attention(t, 0), lambda t: attention(t, 1), up, out_part,
                      lambda t: choose_keys(t, 0), lambda t: choose_keys(t, 1), choose_experts]

            def dots(i, par, t):
                for k in range(TOPK):
                    dve.wait_ge(s_u[k % NU], i * (16 * (TOPK // NU)) + 16 * (k // NU + 1))
                    dve.tensor_tensor_reduce(ubuf[:, k % NU, :], ubuf[:, k % NU, :], h2[:, t, :], 1.0, 0.0,
                                             ALU.mult, ALU.add, adot[:, par, k:k + 1]).then_inc(s_ufree, 1)
                dve.wait_ge(s_gelu, i + 1)
                dve.tensor_tensor(ew[:, par, :], g_sb[:, bass.ds(i * TOPK, TOPK)], gel[:],
                                  ALU.mult).then_inc(s_ew, 1)

            def finish(t):
                dve.wait_ge(s_vfree, NV + (t + 1) * HEADS * TOPK)
                if t:
                    dve.wait_ge(s_stored, 16 * t)
                dve.tensor_tensor(wide[:], ps_y[:], rows[:, 3, :], ALU.mult).then_inc(s_ytaken, 1)
                dve.wait_ge(s_ytaken, t + 1)
                dve.tensor_tensor(wide[:], wide[:], x_sb[:, t, :], ALU.add).then_inc(s_yrow, 1)

            for stage in stages:
                stage(0)
            for i in range(HEADS):
                dots(i, i % 2, 0)
                if i < len(stages):
                    stages[i](1)
            dots(HEADS, 0, 1)
            finish(0)
            dots(HEADS + 1, 1, 1)
            with dve.Fori(1, HEADS // 2) as n:
                for j in range(2):
                    dots(n * 2 + (HEADS + j), j, 1)
            finish(1)

        @block.scalar
        def _(act):
            for n, (src, at) in enumerate(((c, 0), (norm1_g, 8), (norm2_g, 16))):
                act.dma_start(raw[at:at + KD, :], src.rearrange("a (k p) -> (a k) p", p=P)).then_inc(s_small, 16)
            act.dma_start(raw[24:72, :], b_ada.rearrange("a (k p) -> (a k) p", p=P)).then_inc(s_small, 16)
            for n, src in enumerate((fox_q_g, fox_k_g, moba_q_g, moba_k_g)):
                for h in range(2):
                    act.dma_start(raw[72 + n:73 + n, h * HD:(h + 1) * HD], src).then_inc(s_small, 16)
            act.dma_start(bf[:], b_fgate.rearrange("a h -> h a")).then_inc(s_small, 16)
            act.dma_start(wf[:], w_in[0].rearrange("(k p) n -> p k n", p=P)[:, :, F_AT:F_AT + HEADS]) \
               .then_inc(s_small, 16)
            rooted = [0]

            def root(count):
                rooted[0] += 1
                act.wait_ge(s_var, rooted[0])
                act.activation(nrm[:, 2, 0:count], nrm[:, 0, 0:count], ACT.Sqrt).then_inc(s_root, 1)

            await_read(act, "cols")
            act.activation(silu[:], cols[:, 0:KD], ACT.Sigmoid).then_inc(s_sig, 1)
            for t in range(TILES):
                if t == 0:
                    act.wait_ge(s_x, 16)
                act.activation(tmp[:].rearrange("p a n -> p (a n)"), x_sb[:, t, :], ACT.Square,
                               accum_out=ss[:, 0:1]).then_inc(s_sq, 1)
                root(1)
            act.wait_ge(s_fneg, 1)
            act.activation(fx[:, 2, :], fx[:, 1, :], ACT.Exp).then_inc(s_fexp, 1)
            act.wait_ge(s_fone, 1)
            act.activation(fx[:, 1, :], fx[:, 2, :], ACT.Ln).then_inc(s_fln, 1)

            qk_items = [("z", a, b) for a in (QA, KA, QB, KB) for b in range(TILES)]
            qk = 0
            behind = []

            def qk_out():
                c_, t = behind.pop(0)
                key = ("qkT", c_, t)
                await_item(act, key)
                place = (QA, KA, QB, KB).index(c_)
                ins = act.activation(qkT[:, place, :, t * P:(t + 1) * P],
                                     bank(key)[:].rearrange("p (a n) -> p a n", n=P), ACT.Copy,
                                     scale=cols[:, 72 + place:73 + place])
                read(ins, key)

            for c_ in range(NZ):
                for t in range(TILES):
                    key = ("z", c_, t)
                    await_item(act, key)
                    if c_ in (QA, KA, QB, KB):
                        if qk >= 2:
                            await_read(act, qk_items[qk - 2])
                        act.activation(tmp[:, qk % 2, :], bank(key)[:], ACT.Square).then_inc(s_sq, 1)
                        qk += 1
                        root(HEADS)
                        behind.append((c_, t))
                    elif c_ in (VA, VB):
                        read(act.activation(v_sb[:, t, 0 if c_ == VA else 1, :], bank(key)[:], ACT.Copy), key)
                    else:
                        read(act.activation(gates[:, t, c_ - 6, :], bank(key)[:], ACT.Sigmoid), key)
                while behind and behind[0][0] < c_:
                    qk_out()
            while behind:
                qk_out()
            act.wait_ge(s_mod, 1)
            for r in range(4):
                for k in range(KD):
                    n = r * KD + k
                    src = (mod[:, 16 + k:17 + k], a2[:, k:k + 1], mod[:, 24 + k:25 + k], mod[:, 40 + k:41 + k])[r]
                    if n >= ND:
                        o = n - ND
                        await_item(act, ("row", o // KD, o % KD // 4))
                    act.activation(diag[:, n % ND, :], ident[:], ACT.Copy, scale=src).then_inc(s_dg, 1)
            for n in range(4):
                key = ("skT", n)
                await_item(act, key)
                read(act.activation(skT[:, 4 * n:4 * n + 4, :], bank(key)[:].rearrange("p (a n) -> p a n", n=P),
                                    ACT.Copy), key)

            def attention(t, g):
                nk = (t + 1) * P
                n0 = (t * 2 + g) * HEADS
                for s in range(HEADS + 3):
                    if s < HEADS:
                        act.wait_ge(s_sc_max, n0 + s + 1)
                        sl = score[:, s % NS, 0:nk]
                        act.activation(sl, sl, ACT.Exp, bias=mx[:, g, s:s + 1],
                                       accum_out=rsum[:, g, s:s + 1]).then_inc(s_exp, 1)
                    if 0 <= s - 2 < HEADS:
                        h = s - 2
                        key = ("PT", t, g, h)
                        await_item(act, key)
                        read(act.activation(pT[:, h % 2, 0:t + 1, :],
                                            bank(key)[:, 0:nk].rearrange("p (a n) -> p a n", n=P), ACT.Copy), key)
                    if 0 <= s - 3 < HEADS and (s - 3) % 2 == 1:
                        pair = (s - 3) // 2
                        key = ("y", t, g, pair)
                        await_item(act, key)
                        read(act.activation(yT[:, g, pair, :], bank(key)[:, 0:P], ACT.Copy), key)

            def to_tT(t, name):
                for h in range(2):
                    key = (name, t, h)
                    await_item(act, key)
                    read(act.activation(tT[:, 4 * h:4 * h + 4, :],
                                        bank(key)[:].rearrange("p (a n) -> p a n", n=P), ACT.Copy), key)

            def out_part(t):
                act.wait_ge(s_x1, (t + 1) * 4)
                act.activation(tmp[:].rearrange("p a n -> p (a n)"), x_sb[:, t, :], ACT.Square,
                               accum_out=ss[:, 0:1]).then_inc(s_sq, 1)
                root(1)
                to_tT(t, "h2T")

            def scores(t, part):
                for n in range(2 * part, 2 * part + 2):
                    for m in (2 * n, 2 * n + 1):
                        key = ("qp", t, m)
                        await_item(act, key)
                        read(act.activation(qp[:, m % 2, :, :],
                                            bank(key)[:, 0:2 * P].rearrange("p (a n) -> p a n", n=P), ACT.Copy), key)
                    key = ("sc", t, n)
                    await_item(act, key)
                    read(act.activation(sc[:, n * 512:(n + 1) * 512], bank(key)[:], ACT.Copy), key)

            def choice(t):
                act.wait_ge(s_g0, t + 1)
                gt = g_sb[:, t * P:(t + 1) * P]
                act.activation(gt, gt, ACT.Exp).then_inc(s_g1, 1)

            stages = [lambda t: attention(t, 0), lambda t: attention(t, 1), lambda t: to_tT(t, "mixT"), out_part,
                      lambda t: scores(t, 0), lambda t: scores(t, 1), choice]

            def gelu(i, par):
                act.wait_ge(s_ufree, NU + (i + 1) * TOPK)
                if not isinstance(i, int) or i:
                    act.wait_ge(s_ew, i)
                act.activation(gel[:], adot[:, par, :], ACT.Gelu_apprx_tanh).then_inc(s_gelu, 1)

            def diagonals(i, par):
                act.wait_ge(s_ew, i + 1)
                for k in range(TOPK):
                    act.wait_ge(s_vfree, i * TOPK + (k + 1 - ND + NV))
                    act.activation(diag[:, k % ND, :], ident[:], ACT.Copy,
                                   scale=ew[:, par, k:k + 1]).then_inc(s_diag, 1)

            for stage in stages:
                stage(0)
            for i in range(HEADS):
                if i:
                    diagonals(i - 1, (i - 1) % 2)
                gelu(i, i % 2)
                if i < len(stages):
                    stages[i](1)
            for i in (HEADS, HEADS + 1):
                diagonals(i - 1, (i - 1) % 2)
                gelu(i, i % 2)
            with act.Fori(1, HEADS // 2) as n:
                for j in range(2):
                    i = n * 2 + (HEADS + j)
                    diagonals(i - 1, 1 - j)
                    gelu(i, j)
            diagonals(NG - 1, (NG - 1) % 2)

        @block.tensor
        def _(pe):
            def fill(key):
                n = plan[key]
                if n >= NB:
                    pe.wait_ge(s_bank[n % NB], n // NB)
                return banks[n % NB]

            def done(ins):
                return ins.then_inc(s_item, 1)

            def chunk(key):
                n = chunk_no[key]
                pe.wait_ge(s_chunk[n % NW], 16 * (n // NW + 1))
                return ring[:, n % NW, :, :]

            def turn(key, srcs):
                b = fill(key)
                for j, src in enumerate(srcs):
                    ins = pe.transpose(b[:, j * P:(j + 1) * P], src, ident[:])
                done(ins)

            def ada(first, last):
                for n in range(first, last):
                    w = chunk(("ada", n))
                    b = fill(("ada", n))
                    for m in range(4):
                        for k in range(KD):
                            ins = pe.matmul(b[:, m:m + 1], w[:, k, m * P:(m + 1) * P], silu[:, k:k + 1],
                                            start=(k == 0), stop=(k == KD - 1))
                    done(ins)

            pe.wait_ge(s_small, 14 * 16)
            pe.wait_ge(s_const, 1)
            done(pe.transpose(fill("cols")[:, 0:76], raw[0:76, :], ident[0:76, 0:76]))
            pe.wait_ge(s_silu, 1)
            ada(0, ADA_FIRST)
            for t in range(TILES):
                pe.wait_ge(s_xn, t + 1)
                for h in range(2):
                    turn(("xT", t, h), [wide[:, (4 * h + j) * P:(4 * h + j + 1) * P] for j in range(4)])
            for h in range(2):
                for t in range(TILES):
                    await_read(pe, ("xT", t, h))
            turned = 0
            for key in z_order(TILES):
                if key == "f":
                    b = fill(key)
                    for k in range(KD):
                        ins = pe.matmul(b[0:HEADS, 0:T], wf[:, k, :], hT[:, k, :], start=(k == 0), stop=(k == KD - 1))
                    done(ins)
                elif key == "Fcol":
                    pe.wait_ge(s_F, 1)
                    b = fill(key)
                    for t in range(TILES):
                        ins = pe.transpose(b[:, t * HEADS:(t + 1) * HEADS], fx[:, 1, t * P:(t + 1) * P],
                                           ident[0:HEADS, 0:HEADS])
                    done(ins)
                elif key[0] == "z":
                    w = chunk(("z", key[1]))
                    b = fill(key)
                    for k in range(KD):
                        ins = pe.matmul(b[:], hT[:, k, key[2] * P:(key[2] + 1) * P], w[:, k, :],
                                        start=(k == 0), stop=(k == KD - 1))
                    done(ins)
                else:
                    await_read(pe, ("z",) + key[1:])
                    turn(key, [qn[:, turned % 2, j * P:(j + 1) * P] for j in range(4)])
                    turned += 1
            ada(ADA_FIRST, ADA)
            n = 0
            for r in range(4):
                for h in range(2):
                    b = fill(("row", r, h))
                    for j in range(4):
                        n += 1
                        pe.wait_ge(s_dg, n)
                        ins = pe.matmul(b[:, j * P:(j + 1) * P], ones[:], diag[:, (n - 1) % ND, :], start=True, stop=True)
                    done(ins)
            sk = chunk(("sk", 0))
            for n in range(4):
                turn(("skT", n), [sk[:, n, j * P:(j + 1) * P] for j in range(4)])
            pe.wait_ge(s_const, 5)

            def attention(t, g):
                nk = (t + 1) * P
                n0 = (t * 2 + g) * HEADS
                if t == 0 and g == 0:
                    for c_ in (QA, KA, QB, KB):
                        for u in range(TILES):
                            await_read(pe, ("qkT", c_, u))
                    for u in range(TILES):
                        await_read(pe, ("z", VA, u))
                        await_read(pe, ("z", VB, u))
                for s in range(HEADS + 3):
                    if s < HEADS:
                        b = fill(("S", t, g, s))
                        at = HD * (s % 2)
                        q = qkT[at:at + HD, 2 * g, s // 2, t * P:(t + 1) * P]
                        k = qkT[at:at + HD, 2 * g + 1, s // 2, 0:nk]
                        ins = pe.matmul(b[:, 0:nk], q, k, start=True, stop=(g == 1))
                        if g == 0:
                            ins = pe.matmul(b[:, 0:nk], sel[:, s, :], fx[:, 3, 0:nk], start=False, stop=True)
                        done(ins)
                    if 0 <= s - 2 < HEADS:
                        h = s - 2
                        b = fill(("PT", t, g, h))
                        pe.wait_ge(s_prob, n0 + h + 1)
                        for m in range(t + 1):
                            ins = pe.transpose(b[:, m * P:(m + 1) * P], score[:, h % NS, m * P:(m + 1) * P], ident[:])
                        done(ins)
                    if 0 <= s - 3 < HEADS:
                        h = s - 3
                        key = ("y", t, g, h // 2)
                        b = fill(key) if h % 2 == 0 else bank(key)
                        await_read(pe, ("PT", t, g, h))
                        at = HD * (h % 2)
                        for m in range(t + 1):
                            ins = pe.matmul(b[at:at + HD, 0:P], v_sb[:, m, g, h * HD:(h + 1) * HD], pT[:, h % 2, m, :],
                                            start=(m == 0), stop=(m == t))
                        if h % 2 == 1:
                            done(ins)

            def late_chunk(t, key, width):
                no = t * len(late) + late_no[key]
                pe.wait_ge(s_late[no % NL], 16 * (no // NL + 1))
                return late_ring[:, no % NL, :].rearrange("p (k n) -> p k n", n=width)

            def up(t):
                for p_ in range(4):
                    for g in range(2):
                        if p_ == 3:
                            await_read(pe, ("y", t, g, p_))
                for c_ in range(2):
                    for g in range(2):
                        w = late_chunk(t, ("up", c_, g), 512)
                        b = fill(("up", t, c_, g))
                        for k in range(4):
                            ins = pe.matmul(b[:], yT[:, g, k, :], w[:, k, :], start=(k == 0), stop=(k == 3))
                        done(ins)
                for h in range(2):
                    pe.wait_ge(s_xn, TILES + 3 * t + h + 1)
                    turn(("mixT", t, h), [wide[:, (4 * h + j) * P:(4 * h + j + 1) * P] for j in range(4)])

            def out_part(t):
                for h in range(2):
                    await_read(pe, ("mixT", t, h))
                for q in range(4):
                    w = late_chunk(t, ("out", q), 256)
                    b = fill(("o", t, q))
                    for k in range(KD):
                        ins = pe.matmul(b[:, 0:256], tT[:, k, :], w[:, k, :], start=(k == 0), stop=(k == KD - 1))
                    done(ins)
                pe.wait_ge(s_xn, TILES + 3 * t + 3)
                for h in range(2):
                    turn(("h2T", t, h), [h2[:, t, (4 * h + j) * P:(4 * h + j + 1) * P] for j in range(4)])

            def scores(t, part):
                if part == 0:
                    for h in range(2):
                        await_read(pe, ("h2T", t, h))
                for n in range(2 * part, 2 * part + 2):
                    for m in (2 * n, 2 * n + 1):
                        w = late_chunk(t, ("peer", m), 256)
                        b = fill(("qp", t, m))
                        for j in range(2):
                            for k in range(KD):
                                ins = pe.matmul(b[:, j * P:(j + 1) * P], w[:, k, j * P:(j + 1) * P], tT[:, k, :],
                                                start=(k == 0), stop=(k == KD - 1))
                        done(ins)
                    b = fill(("sc", t, n))
                    for m in (2 * n, 2 * n + 1):
                        await_read(pe, ("qp", t, m))
                        for j in range(2):
                            l = 2 * m + j
                            ins = pe.matmul(b[:, (l % 4) * P:(l % 4 + 1) * P], qp[:, m % 2, j, :], skT[:, l, :],
                                            start=True, stop=True)
                    done(ins)

            stages = [lambda t: attention(t, 0), lambda t: attention(t, 1), up, out_part,
                      lambda t: scores(t, 0), lambda t: scores(t, 1)]

            def add_rows(i, first, last):
                for k in range(TOPK):
                    pe.wait_ge(s_diag, i * TOPK + (k + 1))
                    pe.wait_ge(s_v[k % NV], i * (16 * (TOPK // NV)) + 16 * (k // NV + 1))
                    for h in range(2):
                        cut = slice(h * HALF, (h + 1) * HALF)
                        ins = pe.matmul(ps_y[:, cut], diag[:, k % ND, :], vbuf[:, k % NV, cut],
                                        start=(first and k == 0), stop=(last and k == TOPK - 1))
                    ins.then_inc(s_vfree, 1)

            for stage in stages:
                stage(0)
            for i in range(HEADS + 1):
                if i:
                    add_rows(i - 1, i == 1, i == HEADS)
                if i < len(stages):
                    stages[i](1)
            pe.wait_ge(s_ytaken, 1)
            add_rows(HEADS, True, False)
            with pe.Fori(HEADS + 1, NG - 1) as i:
                add_rows(i, False, False)
            add_rows(NG - 1, False, True)


_INS = ["x", "c", "w_ada", "b_ada", "norm1_g", "w_in", "b_fgate", "fox_q_g", "fox_k_g", "moba_q_g", "moba_k_g",
        "w_up_fox", "w_up_moba", "w_out", "norm2_g", "w_peer_q", "peer_sub_keys", "peer_u", "peer_v"]


def kernel(**inputs):
    import numpy as np
    import concourse.bacc as bacc
    from concourse.bass_utils import run_bass_kernel_spmd

    nc = bacc.Bacc("TRN2", target_bir_lowering=False, num_devices=1)
    arrays, args = {}, []
    for name in _INS:
        a = np.ascontiguousarray(inputs[name])
        arrays[f"in_{name}"] = a
        args.append(nc.dram_tensor(f"in_{name}", a.shape, mybir.dt.from_np(a.dtype), kind="ExternalInput").ap())
    out = nc.dram_tensor("out_y", inputs["x"].shape, F32, kind="ExternalOutput").ap()
    block_kernel(nc, *args, out)
    r = run_bass_kernel_spmd(nc, [arrays], core_ids=[0])
    return r.results[0]["out_y"]
```

```python
from contextlib import ExitStack

import concourse.bass as bass
from concourse import mybir

F32 = mybir.dt.float32
U32 = mybir.dt.uint32
I32 = mybir.dt.int32
ALU = mybir.AluOpType
ACT = mybir.ActivationFunctionType
AX_X = mybir.AxisListType.X

P = 128
EPS = 1e-6
NEG = -1e30
HD = 64
HEADS = 8
TOPK = 16
LISTS = 2 * HEADS
WIDE = 4
NARROW = 4
NCAND = WIDE * TOPK + (TOPK - WIDE) * NARROW
NW = 4
NL = 2
NU = 8
NV = 8
ND = 8
NB = 6
NS = 4
QA, KA, VA, QB, KB, VB = range(6)
NZ_QKV = 6
STEPS = HEADS + 3
NZ = 10
ADA = 12
ADA_FIRST = 4
ADA_LATE = {0: 7, 6: 8, 12: 9, 17: 10, 21: 11}


def psum_plan(tiles):
    items = ["cols"] + [("xT", t, h) for t in range(tiles) for h in range(2)]
    items.append("ada_cols")
    items += z_order(tiles)
    for t in range(tiles):
        for g in range(2):
            for s in range(STEPS):
                if s < HEADS:
                    items.append(("S", t, g, s))
                if 0 <= s - 2 < HEADS:
                    items.append(("PT", t, g, s - 2))
                if 0 <= s - 3 < HEADS and (s - 3) % 2 == 1:
                    items.append(("y", t, g, (s - 3) // 2))
                if t == 0 and g * STEPS + s in ADA_LATE:
                    items.append(("ada", ADA_LATE[g * STEPS + s]))
        if t == 0:
            items += [("g2", h) for h in range(2)] + [("skT", n) for n in range(4)]
        for c in range(2):
            items += [("up", t, c, g) for g in range(2)]
        items += [("mixT", t, h) for h in range(2)]
        items += [("o", t, q) for q in range(4)]
        items += [("h2T", t, h) for h in range(2)]
        for n in range(LISTS // 4):
            items += [("qp", t, 2 * n), ("qp", t, 2 * n + 1), ("sc", t, n)]
    return {key: n for n, key in enumerate(items)}


def z_order(tiles):
    items = ["f"]
    behind = []
    for c in range(NZ_QKV):
        items += [("z", c, t) for t in range(tiles)]
        items += behind
        behind = [("qkT", c, t) for t in range(tiles)] if c in (QA, KA, QB, KB) else []
        if c == VA:
            items.append("Fcol")
        if c >= QB:
            items.append(("ada", ADA_FIRST + c - QB))
    return items + behind


def gate_matmuls(u, total):
    return range(u * total // (2 * STEPS), (u + 1) * total // (2 * STEPS))


def block_kernel(nc, x, c, w_ada, b_ada, norm1_g, w_in, b_fgate, fox_q_g, fox_k_g, moba_q_g, moba_k_g,
                 w_up_fox, w_up_moba, w_out, norm2_g, w_peer_q, peer_sub_keys, peer_u, peer_v, out):
    T, D = x.shape[1], x.shape[2]
    TILES = T // P
    KD = D // P
    HALF = D // 2
    NG = TILES * HEADS
    GW = HEADS * HD
    F_AT = 3 * GW
    z_at = [0, GW, 2 * GW] + [F_AT + HEADS + n * GW for n in range(NZ - 3)]
    slopes = [2.0 ** (-8.0 * (h + 1) / HEADS) for h in range(HEADS)]
    plan = psum_plan(TILES)
    assert TILES == 2 and KD == 8 and GW == 512

    chunks = [("ada", n) for n in range(ADA_FIRST)] + [("z", 0), ("z", 1)]
    for n in range(ADA_FIRST, ADA):
        chunks += [("ada", n), ("z", n - ADA_FIRST + 2)]
    chunks.append(("sk", 0))
    chunk_no = {key: n for n, key in enumerate(chunks)}
    late = [("up", c, g) for c in range(2) for g in range(2)]
    late += [("out", n) for n in range(4)] + [("peer", n) for n in range(8)]
    late_no = {key: n for n, key in enumerate(late)}

    with ExitStack() as ctx:
        def sb(name, shape, dt=F32):
            return ctx.enter_context(nc.sbuf_tensor(name, shape, dt))

        def sem(name):
            return ctx.enter_context(nc.semaphore(name))

        ring = sb("ring", [P, NW, KD, 512])
        uv = ring[:].rearrange("p a k n -> p (a k n)").rearrange("p (s d) -> p s d", d=D)
        ubuf, vbuf = uv[:, 0:NU, :], uv[:, NU:NU + NV, :]
        late_ring = sb("late_ring", [P, NL, 2048])
        x_sb = sb("x_sb", [P, TILES, D])
        hT = sb("hT", [P, KD, T])
        sc = hT[:].rearrange("p k t -> p (k t)")
        tT = sb("tT", [P, KD, P])
        qkT = sb("qkT", [P, 4, 4, T])
        v_sb = sb("v_sb", [P, TILES, 2, GW])
        gates = sb("gates", [P, TILES, 4, 512])
        h2 = gates[:, 0, :, :].rearrange("p a n -> p (a n)").rearrange("p (t d) -> p t d", t=TILES)
        rows = sb("rows", [P, 4, D])
        skT = sb("skT", [P, LISTS, P])
        diag = sb("diag", [P, ND, P])
        score = sb("score", [P, NS, T])
        pT = sb("pT", [P, 2, TILES, P])
        tmp = sb("tmp", [P, 2, 512])
        qn = score[:].rearrange("p a n -> p (a n)").rearrange("p (a n) -> p a n", n=512)
        cand = score[:].rearrange("p a n -> p (a n)")[:, 0:HEADS * NCAND].rearrange("p (h n) -> p h n", h=HEADS)
        wide = sb("wide", [P, D])
        yT = sb("yT", [P, 2, 4, P])
        spare = yT[:].rearrange("p a b n -> p (a b n)")
        dist_i = spare[:, 0:T].bitcast(I32)
        pw = spare[:, 0:512].bitcast(U32).rearrange("p (a n) -> p a n", a=4)
        pf = spare[:, 512:1024].rearrange("p (a n) -> p a n", a=4)
        i16f = pT[:].rearrange("p a b n -> p (a b n)")[:, 0:LISTS * TOPK].rearrange("p (l k) -> p l k", k=TOPK)
        qp = sb("qp", [P, 2, 2, P])
        raw = sb("raw", [72, P])
        cols = sb("cols", [P, 72])
        gain = sb("gain", [P, 4])
        sums = wide[:].rearrange("p (a n) -> p a n", a=2)
        silu = sb("silu", [P, KD])
        mod = sb("mod", [P, 16])
        a1 = sb("a1", [P, KD])
        wf = sb("wf", [P, KD, HEADS])
        bf = sb("bf", [HEADS, 1])
        fx = sb("fx", [HEADS, 4, T])
        sel = sb("sel", [HEADS, HEADS, P])
        fcol = sb("fcol", [P, TILES, HEADS])
        ident = sb("ident", [P, P])
        ones = sb("ones", [P, P])
        mask = sb("mask", [P, T])
        dist = sb("dist", [P, T])
        iota_i = sb("iota_i", [P, TOPK], I32)
        iota_f = sb("iota_f", [P, TOPK])
        ss = sb("ss", [P, HEADS])
        nrm = sb("nrm", [P, 4, HEADS])
        mx = sb("mx", [P, 2, HEADS])
        rsum = sb("rsum", [P, 2, HEADS])
        v16 = sb("v16", [P, LISTS, TOPK])
        i16 = sb("i16", [P, LISTS, TOPK], U32)
        tv = sb("tv", [P, HEADS, TOPK])
        pos = sb("pos", [P, HEADS * TOPK], U32)
        gsum = sb("gsum", [P, 2, HEADS])
        g_sb = sb("g_sb", [P, NG * TOPK])
        eid = sb("eid", [P, NG * TOPK], I32)
        idx = sb("idx", [P, 3, TOPK], I32)
        adot = sb("adot", [P, 2, TOPK])
        gel = sb("gel", [P, TOPK])
        ew = sb("ew", [P, 2, TOPK])

        banks = [ctx.enter_context(nc.psum_tensor(f"bank{b}", [P, 512], F32)) for b in range(NB)]
        ps_y = ctx.enter_context(nc.psum_tensor("ps_y", [P, D], F32))

        s_small = sem("small_loaded")
        s_x = sem("x_loaded")
        s_chunk = [sem(f"chunk_landed{n}") for n in range(NW)]
        s_late = [sem(f"late_landed{n}") for n in range(NL)]
        s_misc = sem("gains_and_forget_weights_loaded")
        s_acc = sem("ada_partials_ready")
        s_summed = sem("ada_partials_summed")
        s_a1 = sem("norm1_factors_ready")
        s_gate = sem("gate_product_ready")
        s_gexp = sem("gate_exp_ready")
        s_const = sem("constants_ready")
        s_pool = sem("pool_step")
        s_dve = sem("dve_step")
        s_item = sem("psum_item_ready")
        s_bank = [sem(f"bank_read{b}") for b in range(NB)]
        s_sig = sem("sigmoid_c_ready")
        s_silu = sem("silu_ready")
        s_sq = sem("squares_ready")
        s_var = sem("variance_ready")
        s_root = sem("root_ready")
        s_xn = sem("row_ready_for_transpose")
        s_fneg = sem("minus_abs_f_ready")
        s_fexp = sem("exp_f_ready")
        s_fone = sem("one_plus_exp_ready")
        s_fln = sem("log_ready")
        s_F = sem("F_ready")
        s_dg = sem("column_diagonal_ready")
        s_sc_max = sem("score_max_ready")
        s_exp = sem("exp_ready")
        s_prob = sem("prob_ready")
        s_x1 = sem("x1_ready")
        s_g0 = sem("top_scores_shifted")
        s_g1 = sem("top_scores_exp")
        s_eid = sem("expert_ids_ready")
        s_idx = sem("idx_ready")
        s_free = sem("row_slot_seen_free")
        s_u = [sem(f"u_landed{n}") for n in range(NU)]
        s_v = [sem(f"v_landed{n}") for n in range(NV)]
        s_ufree = sem("u_slots_free")
        s_vfree = sem("v_slots_free")
        s_gelu = sem("gelu_ready")
        s_ew = sem("expert_weights_ready")
        s_diag = sem("diag_ready")
        s_ytaken = sem("y_read")
        s_yrow = sem("y_row_ready")
        s_stored = sem("stored")

        def bank(key):
            return banks[plan[key] % NB]

        def await_item(eng, key):
            eng.wait_ge(s_item, plan[key] + 1)

        def read(ins, key):
            return ins.then_inc(s_bank[plan[key] % NB], 1)

        def await_read(eng, key):
            eng.wait_ge(s_bank[plan[key] % NB], plan[key] // NB + 1)

        def await_chunk_read(eng, n):
            what, m = chunks[n]
            if what == "ada":
                eng.wait_ge(s_acc, m + 1)
            elif m < NZ_QKV:
                await_item(eng, ("z", m, TILES - 1))
            else:
                eng.wait_ge(s_gate, (m - NZ_QKV) * TILES + TILES)

        def gates_done(u):
            return [n // KD for n in gate_matmuls(u, 4 * TILES * KD) if n % KD == KD - 1]

        def late_user(no):
            t, what = no // len(late), late[no % len(late)]
            return {"up": ("up", t) + what[1:], "out": ("o", t) + what[1:], "peer": ("qp", t) + what[1:]}[what[0]]

        block = ctx.enter_context(nc.Block())

        @block.sync
        def _(sp):
            def late_chunk(t, n):
                no = t * len(late) + n
                if no >= NL:
                    await_item(sp, late_user(no - NL))
                what = late[n]
                dst = late_ring[:, no % NL, :]
                if what[0] == "up":
                    src = (w_up_fox, w_up_moba)[what[2]][0].rearrange("(k p) n -> p k n", p=P)
                    src = src[:, :, what[1] * 512:(what[1] + 1) * 512]
                    dst = dst.rearrange("p (k n) -> p k n", n=512)
                else:
                    src = (w_out if what[0] == "out" else w_peer_q)[0].rearrange("(k p) n -> p k n", p=P)
                    src = src[:, :, what[1] * 256:(what[1] + 1) * 256]
                    dst = dst.rearrange("p (k n) -> p k n", n=256)
                sp.dma_start(dst, src).then_inc(s_late[no % NL], 16)

            for src, at in ((c, 0), (norm1_g, 8), (norm2_g, 16)):
                sp.dma_start(raw[at:at + KD, :], src.rearrange("a (k p) -> (a k) p", p=P)).then_inc(s_small, 16)
            sp.dma_start(raw[24:72, :], b_ada.rearrange("a (k p) -> (a k) p", p=P)).then_inc(s_small, 16)
            sp.dma_start(x_sb[:], x[0].rearrange("(t p) d -> p t d", p=P)).then_inc(s_x, 16)
            for n, (what, m) in enumerate(chunks):
                if n >= NW:
                    await_chunk_read(sp, n - NW)
                dst = ring[:, n % NW, :, :]
                if what == "sk":
                    src = peer_sub_keys[0].rearrange("h q n c -> n (h q) c")
                    dst = dst[:, 0:4, :].rearrange("p k (l c) -> p (k l) c", c=P)
                else:
                    w = (w_ada if what == "ada" else w_in)[0].rearrange("(k p) n -> p k n", p=P)
                    at = m * 512 if what == "ada" else z_at[m]
                    src = w[:, :, at:at + 512]
                sp.dma_start(dst, src).then_inc(s_chunk[n % NW], 16)
            for t in range(TILES):
                for n in range(len(late)):
                    late_chunk(t, n)
            for t in range(TILES):
                sp.wait_ge(s_yrow, t + 1)
                sp.dma_start(out[0, t * P:(t + 1) * P, :], wide[:]).then_inc(s_stored, 16)
            sp.wait_ge(s_stored, 16 * TILES)

        @block.gpsimd
        def _(pool):
            pool.memset(ones[:], 1.0).then_inc(s_pool, 1)
            pool.memset(ident[:], 0.0).then_inc(s_pool, 1)
            pool.memset(mask[:], 0.0).then_inc(s_pool, 1)
            pool.memset(sel[:], 0.0).then_inc(s_pool, 1)
            pool.iota(dist_i, pattern=[[-1, T]], base=P, channel_multiplier=1).then_inc(s_pool, 1)
            pool.iota(iota_i[:], pattern=[[1, TOPK]], base=0, channel_multiplier=0).then_inc(s_pool, 1)
            pool.wait_ge(s_pool, 6)
            pool.affine_select(out=ident[:], in_=ident[:], compare_op=ALU.not_equal, fill=1.0, base=0,
                               pattern=[[-1, P]], channel_multiplier=1).then_inc(s_const, 1)
            pool.affine_select(out=mask[:], in_=mask[:], compare_op=ALU.is_ge, fill=NEG, base=P,
                               pattern=[[-1, T]], channel_multiplier=1).then_inc(s_const, 1)
            pool.affine_select(out=sel[:], in_=sel[:], compare_op=ALU.not_equal, fill=1.0, base=0,
                               pattern=[[-1, HEADS], [0, P]], channel_multiplier=1).then_inc(s_const, 1)
            pool.tensor_copy(dist[:], dist_i).then_inc(s_pool, 1)
            pool.tensor_copy(iota_f[:], iota_i[:]).then_inc(s_const, 1)
            pool.wait_ge(s_pool, 7)
            pool.affine_select(out=dist[:], in_=dist[:], compare_op=ALU.is_ge, fill=-NEG, base=P,
                               pattern=[[-1, T]], channel_multiplier=1).then_inc(s_const, 1)

            pool.sem_inc(s_ufree, NU)
            pool.sem_inc(s_vfree, NV)

            def take(i, r):
                pool.wait_ge(s_eid, i + 1)
                pool.sem_inc(s_free, 1)
                pool.tensor_copy(idx[:, r, :], eid[:, bass.ds(i * TOPK, TOPK)]).then_inc(s_idx, 1)
                pool.wait_ge(s_idx, i + 1)
                pool.sem_inc(s_free, 1)

            def fetch_u(i, k, r):
                pool.wait_ge(s_ufree, i * TOPK + k + 1)
                pool.sem_inc(s_free, 1)
                pool.indirect_dma_start(
                    ubuf[:, k % NU, :], None, peer_u[0],
                    bass.IndirectOffsetOnAxis(ap=idx[:, r, k:k + 1], axis=0)).then_inc(s_u[k % NU], 16)

            def fetch_v(i, k, r):
                pool.wait_ge(s_vfree, i * TOPK + k + 1)
                pool.sem_inc(s_free, 1)
                pool.indirect_dma_start(
                    vbuf[:, k % NV, :], None, peer_v[0],
                    bass.IndirectOffsetOnAxis(ap=idx[:, r, k:k + 1], axis=0)).then_inc(s_v[k % NV], 16)

            take(0, 0)
            for k in range(TOPK):
                fetch_u(0, k, 0)
            with pool.Fori(0, (NG - 1) // 3) as n:
                for j in range(3):
                    i = n * 3 + (1 + j)
                    take(i, (j + 1) % 3)
                    for k in range(TOPK):
                        fetch_u(i, k, (j + 1) % 3)
                        fetch_v(i - 1, k, j)
            for k in range(TOPK):
                fetch_v(NG - 1, k, 0)

        @block.vector
        def _(dve):
            steps = [0]

            def link(ins):
                steps[0] += 1
                ins.then_inc(s_dve, 1)
                dve.wait_ge(s_dve, steps[0])

            roots = [0]
            squares = [0]

            def inverse_root(n, count):
                v, r, q, m = (nrm[:, j, 0:count] for j in range(4))
                roots[0] += 1
                dve.tensor_scalar(v, ss[:, 0:count], 1.0 / n, EPS, ALU.mult, ALU.add).then_inc(s_var, 1)
                dve.wait_ge(s_root, roots[0])
                link(dve.reciprocal(r, q))
                link(dve.tensor_tensor(m, r, r, ALU.mult))
                link(dve.tensor_tensor(m, m, v, ALU.mult))
                link(dve.tensor_scalar(m, m, -0.5, 1.5, ALU.mult, ALU.add))
                link(dve.tensor_tensor(v, r, m, ALU.mult))

            def partials(first, last):
                for j in range(first, last):
                    n, k = j // KD, j % KD
                    acc = sums[:, n % 2, :]
                    no = chunk_no["ada", n]
                    w = ring[:, no % NW, k, :]
                    if k == 0:
                        dve.wait_ge(s_chunk[no % NW], 16 * (no // NW + 1))
                        if n >= ADA_FIRST + 2:
                            await_item(dve, ("ada", n - 2))
                        elif n == ADA_FIRST + 1:
                            await_item(dve, "ada_cols")
                        elif n >= 2:
                            dve.wait_ge(s_summed, n - 1)
                        link(dve.tensor_scalar(acc, w, silu[:, 0:1], None, ALU.mult))
                        continue
                    link(dve.scalar_tensor_tensor(out=acc, in0=w, scalar=silu[:, k:k + 1], in1=acc,
                                                  op0=ALU.mult, op1=ALU.add))
                    if k == KD - 1:
                        for m in range(4):
                            part = acc[:, m * P:(m + 1) * P]
                            at = 24 + 4 * n + m
                            ins = dve.scalar_tensor_tensor(out=part, in0=ident[:], scalar=cols[:, at:at + 1],
                                                           in1=part, op0=ALU.mult, op1=ALU.add)
                        ins.then_inc(s_acc, 1)

            await_item(dve, "cols")
            read(dve.tensor_copy(cols[:], bank("cols")[:, 0:72]), "cols")
            await_read(dve, "cols")
            dve.wait_ge(s_sig, 1)
            dve.tensor_tensor(silu[:], silu[:], cols[:, 0:KD], ALU.mult).then_inc(s_silu, 1)
            dve.wait_ge(s_silu, 1)

            for t in range(TILES):
                dve.wait_ge(s_sq, t + 1)
                inverse_root(D, 1)
                if t:
                    await_item(dve, ("xT", t - 1, 1))
                dve.tensor_scalar(wide[:], x_sb[:, t, :], nrm[:, 0, 0:1], None, ALU.mult).then_inc(s_xn, 1)
                dve.wait_ge(s_xn, t + 1)
            await_item(dve, ("xT", TILES - 1, 1))
            partials(0, ADA_FIRST * KD)
            await_item(dve, "ada_cols")
            read(dve.tensor_copy(mod[:], bank("ada_cols")[:, 0:4 * ADA_FIRST]), "ada_cols")
            await_read(dve, "ada_cols")
            dve.scalar_tensor_tensor(out=a1[:], in0=mod[:, 8:16], scalar=1.0, in1=cols[:, 8:16],
                                     op0=ALU.add, op1=ALU.mult).then_inc(s_a1, 1)
            dve.wait_ge(s_a1, 1)
            for h in range(2):
                key = ("xT", 0, h)
                for k in range(4 * h, 4 * h + 4):
                    ins = dve.tensor_scalar(hT[:, k, 0:P], bank(key)[:, (k % 4) * P:(k % 4 + 1) * P],
                                            a1[:, k:k + 1], mod[:, k:k + 1], ALU.mult, ALU.add)
                read(ins, key)
            dve.wait_ge(s_misc, 10 * 16)
            for n in (0, 2):
                link(dve.tensor_scalar(gain[:, n:n + 1], gain[:, n:n + 1], HD ** -0.5, None, ALU.mult))

            def forget_gates():
                xs, a, b, neg = (fx[:, n, :] for n in range(4))
                await_item(dve, "f")
                read(dve.tensor_scalar(xs, bank("f")[0:HEADS, 0:T], bf[:, 0:1], None, ALU.add), "f")
                await_read(dve, "f")
                link(dve.scalar_tensor_tensor(out=a, in0=xs, scalar=-1.0, in1=xs, op0=ALU.mult, op1=ALU.min))
                dve.tensor_scalar(xs, xs, 0.0, None, ALU.min).then_inc(s_fneg, 1)
                dve.wait_ge(s_fneg, 1)
                dve.wait_ge(s_fexp, 1)
                dve.tensor_scalar(b, b, 1.0, None, ALU.add).then_inc(s_fone, 1)
                dve.wait_ge(s_fln, 1)
                link(dve.tensor_tensor(xs, xs, a, ALU.subtract))
                link(dve.memset(b, 1.0))
                link(dve.tensor_tensor_scan(a, b, xs, 0.0, ALU.mult, ALU.add))
                dve.tensor_scalar(neg, a, -1.0, None, ALU.mult).then_inc(s_F, 1)

            forget_gates()
            norms = 0
            for c_ in range(NZ_QKV):
                if c_ >= QB:
                    n = ADA_FIRST + c_ - QB
                    partials(n * KD, (n + 1) * KD)
                if c_ == QB:
                    await_item(dve, "Fcol")
                    dve.tensor_copy(fcol[:].rearrange("p t h -> p (t h)"),
                                    bank("Fcol")[:, 0:TILES * HEADS]).then_inc(s_bank[plan["Fcol"] % NB], 1)
                if c_ not in (QA, KA, QB, KB):
                    continue
                for t in range(TILES):
                    key = ("z", c_, t)
                    dve.wait_ge(s_sq, TILES + norms + 1)
                    link(dve.tensor_reduce(ss[:], tmp[:, norms % 2, :].rearrange("p (h d) -> p h d", d=HD),
                                           AX_X, ALU.add))
                    inverse_root(HD, HEADS)
                    if norms >= 2:
                        pc, pt = [(a, b) for a in (QA, KA, QB, KB) for b in range(TILES)][norms - 2]
                        await_item(dve, ("qkT", pc, pt))
                    ins = dve.tensor_tensor(
                        qn[:, norms % 2, :].rearrange("p (h d) -> p h d", d=HD),
                        bank(key)[:].rearrange("p (h d) -> p h d", d=HD),
                        nrm[:, 0, :].unsqueeze(2).to_broadcast([P, HEADS, HD]), ALU.mult)
                    read(ins, key)
                    norms += 1
            def between(u):
                first = (ADA_LATE[0] + 1) * KD
                steps_ = ADA * KD - first
                partials(first + u * steps_ // (2 * STEPS - 1) if u else first,
                         first + min(u + 1, 2 * STEPS - 1) * steps_ // (2 * STEPS - 1))
                for m in gates_done(u - 1) if u else ():
                    gate(m)

            def gate(m):
                z = gates[:, m % TILES, m // TILES, :]
                dve.wait_ge(s_gexp, m + 1)
                link(dve.tensor_scalar(z, z, 1.0, None, ALU.add))
                link(dve.reciprocal(z, z))

            def finish_setup():
                for m in gates_done(2 * STEPS - 1):
                    gate(m)
                for n in (8, 9):
                    await_read(dve, ("ada", n))
                for h in range(2):
                    key = ("g2", h)
                    await_item(dve, key)
                    cut = slice(h * HALF, (h + 1) * HALF)
                    read(dve.scalar_tensor_tensor(out=rows[:, 1, cut], in0=rows[:, 1, cut], scalar=1.0,
                                                  in1=bank(key)[:], op0=ALU.add, op1=ALU.mult), key)
                    await_read(dve, key)
                await_item(dve, ("ada", ADA - 1))

            def attention(t, g):
                nk = (t + 1) * P
                n0 = (t * 2 + g) * HEADS
                par = g
                for s in range(STEPS):
                    if s < HEADS:
                        key = ("S", t, g, s)
                        sl = score[:, s % NS, 0:nk]
                        await_item(dve, key)
                        if n0 + s >= NS:
                            o = n0 + s - NS
                            await_item(dve, ("PT", o // (2 * HEADS), o // HEADS % 2, o % HEADS))
                        if g == 0:
                            ins = dve.scalar_tensor_tensor(out=sl, in0=bank(key)[:, 0:nk], scalar=fcol[:, t, s:s + 1],
                                                           in1=mask[:, T - nk:T], op0=ALU.add, op1=ALU.add)
                        else:
                            ins = dve.scalar_tensor_tensor(out=sl, in0=dist[:, T - nk:T], scalar=-slopes[s],
                                                           in1=bank(key)[:, 0:nk], op0=ALU.mult, op1=ALU.add)
                        read(ins, key)
                        await_read(dve, key)
                        link(dve.tensor_reduce(mx[:, par, s:s + 1], sl, AX_X, ALU.max))
                        dve.tensor_scalar(mx[:, par, s:s + 1], mx[:, par, s:s + 1], -1.0, None,
                                          ALU.mult).then_inc(s_sc_max, 1)
                    if 1 <= s <= HEADS:
                        o = s - 1
                        dve.wait_ge(s_exp, n0 + o + 1)
                        link(dve.reciprocal(rsum[:, par, o:o + 1], rsum[:, par, o:o + 1]))
                        po = score[:, o % NS, 0:nk]
                        dve.tensor_scalar(po, po, rsum[:, par, o:o + 1], None, ALU.mult).then_inc(s_prob, 1)
                    if t == 0:
                        between(g * STEPS + s)

            def up(t):
                for c_ in range(2):
                    for g in range(2):
                        key = ("up", t, c_, g)
                        await_item(dve, key)
                        read(dve.tensor_tensor(tmp[:, g, :], gates[:, t, 2 * g + c_, :], bank(key)[:], ALU.mult), key)
                        await_read(dve, key)
                    dve.tensor_tensor(wide[:, c_ * 512:(c_ + 1) * 512], tmp[:, 0, :], tmp[:, 1, :],
                                      ALU.add).then_inc(s_xn, 1)
                    dve.wait_ge(s_xn, TILES + t * 3 + c_ + 1)

            def out_part(t):
                for q in range(4):
                    key = ("o", t, q)
                    cut = slice(q * 256, (q + 1) * 256)
                    await_item(dve, key)
                    read(dve.tensor_tensor(tmp[:, q % 2, 0:256], bank(key)[:, 0:256], rows[:, 0, cut], ALU.mult), key)
                    await_read(dve, key)
                    dve.tensor_tensor(x_sb[:, t, cut], x_sb[:, t, cut], tmp[:, q % 2, 0:256],
                                      ALU.add).then_inc(s_x1, 1)
                    dve.wait_ge(s_x1, t * 4 + q + 1)
                dve.wait_ge(s_sq, TILES + 4 * TILES + t + 1)
                inverse_root(D, 1)
                link(dve.scalar_tensor_tensor(out=h2[:, t, :], in0=x_sb[:, t, :], scalar=nrm[:, 0, 0:1],
                                              in1=rows[:, 1, :], op0=ALU.mult, op1=ALU.mult))
                dve.tensor_tensor(h2[:, t, :], h2[:, t, :], rows[:, 2, :], ALU.add).then_inc(s_xn, 1)
                dve.wait_ge(s_xn, TILES + t * 3 + 3)

            def top16(values, indices, scores, n):
                for half in range(2):
                    cut = slice(8 * half, 8 * half + 8)
                    for l in range(n):
                        ins = dve.max(values(l)[:, cut], scores(l))
                    link(ins)
                    for l in range(n):
                        ins = dve.max_index(indices(l)[:, cut], values(l)[:, cut], scores(l))
                    link(ins)
                    if half == 0:
                        for l in range(n):
                            ins = dve.match_replace(scores(l), values(l)[:, cut], scores(l), -3.0e38)
                        link(ins)

            def choose_keys(t, part):
                for n in (2 * part, 2 * part + 1):
                    await_read(dve, ("sc", t, n))
                top16(lambda l: v16[:, part * 8 + l, :], lambda l: i16[:, part * 8 + l, :],
                      lambda l: sc[:, (part * 8 + l) * P:(part * 8 + l + 1) * P], 8)

            def choose_experts(t, part):
                nh = HEADS // 2
                nk = nh * TOPK
                lists = slice(part * 2 * nh, (part + 1) * 2 * nh)
                s1 = v16[:, lists, :].rearrange("p (h q) k -> p h q k", q=2)
                link(dve.tensor_copy(i16f[:, lists, :], i16[:, lists, :]))
                cd = cand[:, part * nh:(part + 1) * nh, :]
                c1 = cd[:, :, 0:WIDE * TOPK].rearrange("p h (a b) -> p h a b", b=TOPK)
                c2 = cd[:, :, WIDE * TOPK:NCAND].rearrange("p h (a b) -> p h a b", b=NARROW)
                link(dve.tensor_tensor(c1, s1[:, :, 0, 0:WIDE].unsqueeze(3).to_broadcast([P, nh, WIDE, TOPK]),
                                       s1[:, :, 1, :].unsqueeze(2).to_broadcast([P, nh, WIDE, TOPK]), ALU.add))
                link(dve.tensor_tensor(
                    c2, s1[:, :, 0, WIDE:TOPK].unsqueeze(3).to_broadcast([P, nh, TOPK - WIDE, NARROW]),
                    s1[:, :, 1, 0:NARROW].unsqueeze(2).to_broadcast([P, nh, TOPK - WIDE, NARROW]), ALU.add))
                p3 = pos[:, 0:nk].rearrange("p (h k) -> p h k", k=TOPK)
                tp = tv[:, 0:nh, :]
                top16(lambda l: tp[:, l, :], lambda l: p3[:, l, :], lambda l: cd[:, l, :], nh)
                at = t * P + part * nk
                gt = g_sb[:, at:at + nk].rearrange("p (h k) -> p h k", k=TOPK)
                dve.tensor_tensor(gt, tp, tp[:, :, 0:1].to_broadcast([P, nh, TOPK]),
                                  ALU.subtract).then_inc(s_g0, 1)
                lo, hi, l2, h2_ = (pw[:, n, 0:nk] for n in range(4))
                af, bf_, m, d = (pf[:, n, 0:nk] for n in range(4))
                ps = pos[:, 0:nk]
                link(dve.tensor_scalar(hi, ps, 4, None, ALU.logical_shift_right))
                link(dve.tensor_scalar(lo, ps, TOPK - 1, None, ALU.bitwise_and))
                link(dve.tensor_scalar(h2_, ps, 2, None, ALU.logical_shift_right))
                link(dve.tensor_scalar(l2, ps, NARROW - 1, None, ALU.bitwise_and))
                link(dve.tensor_scalar(m, ps, float(WIDE * TOPK), None, ALU.is_ge))
                link(dve.scalar_tensor_tensor(out=d, in0=h2_, scalar=float(WIDE - WIDE * TOPK // NARROW), in1=hi,
                                              op0=ALU.add, op1=ALU.subtract))
                link(dve.tensor_tensor(d, d, m, ALU.mult))
                link(dve.tensor_tensor(af, d, hi, ALU.add))
                link(dve.tensor_tensor(d, l2, lo, ALU.subtract))
                link(dve.tensor_tensor(d, d, m, ALU.mult))
                link(dve.tensor_tensor(bf_, d, lo, ALU.add))
                ii = i16f[:, lists, :].rearrange("p (h q) k -> p h q k", q=2)
                place = sc[:, part * nk * TOPK:(part + 1) * nk * TOPK]
                oh = place.rearrange("p (h k r) -> p h k r", h=nh, k=TOPK)
                oh2 = place.rearrange("p (k r) -> p k r", r=TOPK)
                for rank, q, to in ((af, 0, m), (bf_, 1, d)):
                    link(dve.tensor_tensor(oh2, rank.unsqueeze(2).to_broadcast([P, nk, TOPK]),
                                           iota_f[:].unsqueeze(1).to_broadcast([P, nk, TOPK]), ALU.is_equal))
                    link(dve.tensor_tensor(oh, oh, ii[:, :, q, :].unsqueeze(2).to_broadcast([P, nh, TOPK, TOPK]),
                                           ALU.mult))
                    link(dve.tensor_reduce(to, oh2, AX_X, ALU.add))
                dve.scalar_tensor_tensor(out=eid[:, at:at + nk], in0=m, scalar=float(P), in1=d,
                                         op0=ALU.mult, op1=ALU.add).then_inc(s_eid, nh)
                dve.wait_ge(s_g1, 2 * t + part + 1)
                link(dve.tensor_reduce(gsum[:, 0, 0:nh], gt, AX_X, ALU.add))
                link(dve.reciprocal(gsum[:, 1, 0:nh], gsum[:, 0, 0:nh]))
                link(dve.tensor_tensor(gt, gt, gsum[:, 1, 0:nh].unsqueeze(2).to_broadcast([P, nh, TOPK]), ALU.mult))

            after = {0: lambda: choose_experts(0, 1),
                     1: lambda: attention(1, 0), 2: lambda: attention(1, 1), 3: lambda: up(1),
                     4: lambda: out_part(1), 5: lambda: choose_keys(1, 0), 6: lambda: choose_experts(1, 0),
                     7: lambda: None,
                     8: lambda: choose_keys(1, 1), 9: lambda: choose_experts(1, 1)}

            def dots(i, par, t):
                for k in range(TOPK):
                    dve.wait_ge(s_u[k % NU], i * (16 * (TOPK // NU)) + 16 * (k // NU + 1))
                    dve.tensor_tensor_reduce(ubuf[:, k % NU, :], ubuf[:, k % NU, :], h2[:, t, :], 1.0, 0.0,
                                             ALU.mult, ALU.add, adot[:, par, k:k + 1]).then_inc(s_ufree, 1)
                dve.wait_ge(s_gelu, i + 1)
                dve.tensor_tensor(ew[:, par, :], g_sb[:, bass.ds(i * TOPK, TOPK)], gel[:],
                                  ALU.mult).then_inc(s_ew, 1)

            def finish(t):
                dve.wait_ge(s_vfree, NV + (t + 1) * HEADS * TOPK)
                if t:
                    dve.wait_ge(s_stored, 16 * t)
                dve.tensor_tensor(wide[:], ps_y[:], rows[:, 3, :], ALU.mult).then_inc(s_ytaken, 1)
                dve.wait_ge(s_ytaken, t + 1)
                dve.tensor_tensor(wide[:], wide[:], x_sb[:, t, :], ALU.add).then_inc(s_yrow, 1)

            partials(ADA_LATE[0] * KD, (ADA_LATE[0] + 1) * KD)
            attention(0, 0)
            attention(0, 1)
            finish_setup()
            up(0)
            out_part(0)
            choose_keys(0, 0)
            choose_experts(0, 0)
            choose_keys(0, 1)
            for i in range(HEADS):
                dots(i, i % 2, 0)
                after[i]()
            dots(HEADS, 0, 1)
            finish(0)
            after[HEADS]()
            dots(HEADS + 1, 1, 1)
            after[HEADS + 1]()
            with dve.Fori(1, HEADS // 2) as n:
                for j in range(2):
                    dots(n * 2 + (HEADS + j), j, 1)
            finish(1)

        @block.scalar
        def _(act):
            for n, src in enumerate((fox_q_g, fox_k_g, moba_q_g, moba_k_g)):
                for h in range(2):
                    act.dma_start(gain[h * HD:(h + 1) * HD, n:n + 1], src.rearrange("a d -> d a")) \
                       .then_inc(s_misc, 16)
            act.dma_start(bf[:], b_fgate.rearrange("a h -> h a")).then_inc(s_misc, 16)
            act.dma_start(wf[:], w_in[0].rearrange("(k p) n -> p k n", p=P)[:, :, F_AT:F_AT + HEADS]) \
               .then_inc(s_misc, 16)
            rooted = [0]

            def root(count):
                rooted[0] += 1
                act.wait_ge(s_var, rooted[0])
                act.activation(nrm[:, 2, 0:count], nrm[:, 0, 0:count], ACT.Sqrt).then_inc(s_root, 1)

            await_read(act, "cols")
            act.activation(silu[:], cols[:, 0:KD], ACT.Sigmoid).then_inc(s_sig, 1)
            for t in range(TILES):
                if t == 0:
                    act.wait_ge(s_x, 16)
                act.activation(tmp[:].rearrange("p a n -> p (a n)"), x_sb[:, t, :], ACT.Square,
                               accum_out=ss[:, 0:1]).then_inc(s_sq, 1)
                root(1)
            act.wait_ge(s_a1, 1)
            for t in range(1, TILES):
                for h in range(2):
                    key = ("xT", t, h)
                    for k in range(4 * h, 4 * h + 4):
                        ins = act.activation(hT[:, k, t * P:(t + 1) * P], bank(key)[:, (k % 4) * P:(k % 4 + 1) * P],
                                             ACT.Identity, scale=a1[:, k:k + 1], bias=mod[:, k:k + 1])
                    read(ins, key)
            act.wait_ge(s_fneg, 1)
            act.activation(fx[:, 2, :], fx[:, 1, :], ACT.Exp).then_inc(s_fexp, 1)
            act.wait_ge(s_fone, 1)
            act.activation(fx[:, 1, :], fx[:, 2, :], ACT.Ln).then_inc(s_fln, 1)

            qk_items = [("z", a, b) for a in (QA, KA, QB, KB) for b in range(TILES)]
            qk = 0
            behind = []

            def qk_out():
                c_, t = behind.pop(0)
                key = ("qkT", c_, t)
                await_item(act, key)
                place = (QA, KA, QB, KB).index(c_)
                ins = act.activation(qkT[:, place, :, t * P:(t + 1) * P],
                                     bank(key)[:].rearrange("p (a n) -> p a n", n=P), ACT.Copy,
                                     scale=gain[:, place:place + 1])
                read(ins, key)

            def row_out(n):
                key = ("ada", n)
                await_item(act, key)
                r, h = (0, 2, 1, 3)[(n - ADA_FIRST) // 2], n % 2
                read(act.activation(rows[:, r, h * HALF:(h + 1) * HALF], bank(key)[:], ACT.Copy), key)

            for c_ in range(NZ_QKV):
                for t in range(TILES):
                    key = ("z", c_, t)
                    await_item(act, key)
                    if c_ in (QA, KA, QB, KB):
                        if qk >= 2:
                            await_read(act, qk_items[qk - 2])
                        act.activation(tmp[:, qk % 2, :], bank(key)[:], ACT.Square).then_inc(s_sq, 1)
                        qk += 1
                        root(HEADS)
                        behind.append((c_, t))
                    else:
                        read(act.activation(v_sb[:, t, 0 if c_ == VA else 1, :], bank(key)[:], ACT.Copy), key)
                while behind and behind[0][0] < c_:
                    qk_out()
                if c_ >= QB:
                    row_out(ADA_FIRST + c_ - QB)
            while behind:
                qk_out()
            def between(u):
                if u in ADA_LATE:
                    row_out(ADA_LATE[u])
                for m in gates_done(u):
                    act.wait_ge(s_gate, m + 1)
                    act.activation(gates[:, m % TILES, m // TILES, :], ps_y[:, (m % 2) * 512:(m % 2 + 1) * 512],
                                   ACT.Exp, scale=-1.0).then_inc(s_gexp, 1)

            def finish_setup():
                for k in range(KD):
                    act.activation(diag[:, k, :], ident[:], ACT.Copy, scale=cols[:, 16 + k:17 + k]).then_inc(s_dg, 1)
                for n in range(4):
                    key = ("skT", n)
                    await_item(act, key)
                    read(act.activation(skT[:, 4 * n:4 * n + 4, :], bank(key)[:].rearrange("p (a n) -> p a n", n=P),
                                        ACT.Copy), key)

            def attention(t, g):
                nk = (t + 1) * P
                n0 = (t * 2 + g) * HEADS
                for s in range(STEPS):
                    if s < HEADS:
                        act.wait_ge(s_sc_max, n0 + s + 1)
                        sl = score[:, s % NS, 0:nk]
                        act.activation(sl, sl, ACT.Exp, bias=mx[:, g, s:s + 1],
                                       accum_out=rsum[:, g, s:s + 1]).then_inc(s_exp, 1)
                    if 0 <= s - 2 < HEADS:
                        h = s - 2
                        key = ("PT", t, g, h)
                        await_item(act, key)
                        read(act.activation(pT[:, h % 2, 0:t + 1, :],
                                            bank(key)[:, 0:nk].rearrange("p (a n) -> p a n", n=P), ACT.Copy), key)
                    if 0 <= s - 3 < HEADS and (s - 3) % 2 == 1:
                        pair = (s - 3) // 2
                        key = ("y", t, g, pair)
                        await_item(act, key)
                        read(act.activation(yT[:, g, pair, :], bank(key)[:, 0:P], ACT.Copy), key)
                    if t == 0:
                        between(g * STEPS + s)

            def to_tT(t, name):
                for h in range(2):
                    key = (name, t, h)
                    await_item(act, key)
                    read(act.activation(tT[:, 4 * h:4 * h + 4, :],
                                        bank(key)[:].rearrange("p (a n) -> p a n", n=P), ACT.Copy), key)

            def out_part(t):
                act.wait_ge(s_x1, (t + 1) * 4)
                act.activation(tmp[:].rearrange("p a n -> p (a n)"), x_sb[:, t, :], ACT.Square,
                               accum_out=ss[:, 0:1]).then_inc(s_sq, 1)
                root(1)
                to_tT(t, "h2T")

            def scores(t, part):
                for n in range(2 * part, 2 * part + 2):
                    for m in (2 * n, 2 * n + 1):
                        key = ("qp", t, m)
                        await_item(act, key)
                        read(act.activation(qp[:, m % 2, :, :],
                                            bank(key)[:, 0:2 * P].rearrange("p (a n) -> p a n", n=P), ACT.Copy), key)
                    key = ("sc", t, n)
                    await_item(act, key)
                    read(act.activation(sc[:, n * 512:(n + 1) * 512], bank(key)[:], ACT.Copy), key)

            def choice(t, part):
                act.wait_ge(s_g0, 2 * t + part + 1)
                at = (2 * t + part) * (P // 2)
                gt = g_sb[:, at:at + P // 2]
                act.activation(gt, gt, ACT.Exp).then_inc(s_g1, 1)

            after = {0: lambda: choice(0, 1),
                     1: lambda: attention(1, 0), 2: lambda: attention(1, 1), 3: lambda: to_tT(1, "mixT"),
                     4: lambda: out_part(1), 5: lambda: scores(1, 0),
                     6: lambda: (scores(1, 1), choice(1, 0)), 7: lambda: None,
                     8: lambda: None, 9: lambda: choice(1, 1)}

            def gelu(i, par):
                act.wait_ge(s_ufree, NU + (i + 1) * TOPK)
                if not isinstance(i, int) or i:
                    act.wait_ge(s_ew, i)
                act.activation(gel[:], adot[:, par, :], ACT.Gelu_apprx_tanh).then_inc(s_gelu, 1)

            def diagonals(i, par):
                act.wait_ge(s_ew, i + 1)
                for k in range(TOPK):
                    act.wait_ge(s_vfree, i * TOPK + (k + 1 - ND + NV))
                    act.activation(diag[:, k % ND, :], ident[:], ACT.Copy,
                                   scale=ew[:, par, k:k + 1]).then_inc(s_diag, 1)

            attention(0, 0)
            attention(0, 1)
            finish_setup()
            to_tT(0, "mixT")
            out_part(0)
            scores(0, 0)
            scores(0, 1)
            choice(0, 0)
            for i in range(HEADS + 2):
                if i:
                    diagonals(i - 1, (i - 1) % 2)
                gelu(i, i % 2)
                after[i]()
            with act.Fori(1, HEADS // 2) as n:
                for j in range(2):
                    i = n * 2 + (HEADS + j)
                    diagonals(i - 1, 1 - j)
                    gelu(i, j)
            diagonals(NG - 1, (NG - 1) % 2)

        @block.tensor
        def _(pe):
            def fill(key):
                n = plan[key]
                if n >= NB:
                    pe.wait_ge(s_bank[n % NB], n // NB)
                return banks[n % NB]

            def done(ins):
                return ins.then_inc(s_item, 1)

            def chunk(key):
                n = chunk_no[key]
                pe.wait_ge(s_chunk[n % NW], 16 * (n // NW + 1))
                return ring[:, n % NW, :, :]

            def turn(key, srcs):
                b = fill(key)
                for j, src in enumerate(srcs):
                    ins = pe.transpose(b[:, j * P:(j + 1) * P], src, ident[:])
                done(ins)

            def ada_row(n):
                pe.wait_ge(s_acc, n + 1)
                done(pe.matmul(fill(("ada", n))[:], ones[:], sums[:, n % 2, :], start=True, stop=True))

            pe.wait_ge(s_small, 4 * 16)
            pe.wait_ge(s_const, 1)
            done(pe.transpose(fill("cols")[:, 0:72], raw[:], ident[0:72, 0:72]))
            for t in range(TILES):
                pe.wait_ge(s_xn, t + 1)
                for h in range(2):
                    turn(("xT", t, h), [wide[:, (4 * h + j) * P:(4 * h + j + 1) * P] for j in range(4)])
            b = fill("ada_cols")
            for n in range(ADA_FIRST):
                pe.wait_ge(s_acc, n + 1)
                for m in range(4):
                    ins = pe.matmul(b[:, 4 * n + m:4 * n + m + 1], sums[:, n % 2, m * P:(m + 1) * P], ones[:, 0:1],
                                    start=True, stop=True)
                if n < ADA_FIRST - 1:
                    ins.then_inc(s_summed, 1)
            done(ins)
            for h in range(2):
                for t in range(TILES):
                    await_read(pe, ("xT", t, h))
            pe.wait_ge(s_misc, 10 * 16)
            turned = 0
            for key in z_order(TILES):
                if key == "f":
                    b = fill(key)
                    for k in range(KD):
                        ins = pe.matmul(b[0:HEADS, 0:T], wf[:, k, :], hT[:, k, :], start=(k == 0), stop=(k == KD - 1))
                    done(ins)
                elif key == "Fcol":
                    pe.wait_ge(s_F, 1)
                    b = fill(key)
                    for t in range(TILES):
                        ins = pe.transpose(b[:, t * HEADS:(t + 1) * HEADS], fx[:, 1, t * P:(t + 1) * P],
                                           ident[0:HEADS, 0:HEADS])
                    done(ins)
                elif key[0] == "ada":
                    ada_row(key[1])
                elif key[0] == "z":
                    w = chunk(("z", key[1]))
                    b = fill(key)
                    for k in range(KD):
                        ins = pe.matmul(b[:], hT[:, k, key[2] * P:(key[2] + 1) * P], w[:, k, :],
                                        start=(k == 0), stop=(k == KD - 1))
                    done(ins)
                else:
                    await_read(pe, ("z",) + key[1:])
                    turn(key, [qn[:, turned % 2, j * P:(j + 1) * P] for j in range(4)])
                    turned += 1
            def between(u):
                if u in ADA_LATE:
                    ada_row(ADA_LATE[u])
                for n in gate_matmuls(u, 4 * TILES * KD):
                    m, k = n // KD, n % KD
                    if k == 0:
                        w = chunk(("z", NZ_QKV + m // TILES))
                        if m >= 2:
                            pe.wait_ge(s_gexp, m - 1)
                    else:
                        no = chunk_no["z", NZ_QKV + m // TILES]
                        w = ring[:, no % NW, :, :]
                    ins = pe.matmul(ps_y[:, (m % 2) * 512:(m % 2 + 1) * 512], hT[:, k, (m % TILES) * P:(m % TILES + 1) * P],
                                    w[:, k, :], start=(k == 0), stop=(k == KD - 1))
                    if k == KD - 1:
                        ins.then_inc(s_gate, 1)

            def finish_setup():
                for h in range(2):
                    pe.wait_ge(s_dg, 4 * h + 4)
                    b = fill(("g2", h))
                    for j in range(4):
                        ins = pe.matmul(b[:, j * P:(j + 1) * P], ones[:], diag[:, 4 * h + j, :], start=True, stop=True)
                    done(ins)
                sk = chunk(("sk", 0))
                for n in range(4):
                    turn(("skT", n), [sk[:, n, j * P:(j + 1) * P] for j in range(4)])

            pe.wait_ge(s_const, 5)

            def attention(t, g):
                nk = (t + 1) * P
                n0 = (t * 2 + g) * HEADS
                if t == 0 and g == 0:
                    for c_ in (QA, KA, QB, KB):
                        for u in range(TILES):
                            await_read(pe, ("qkT", c_, u))
                    for u in range(TILES):
                        await_read(pe, ("z", VA, u))
                        await_read(pe, ("z", VB, u))
                for s in range(STEPS):
                    if s < HEADS:
                        b = fill(("S", t, g, s))
                        at = HD * (s % 2)
                        q = qkT[at:at + HD, 2 * g, s // 2, t * P:(t + 1) * P]
                        k = qkT[at:at + HD, 2 * g + 1, s // 2, 0:nk]
                        ins = pe.matmul(b[:, 0:nk], q, k, start=True, stop=(g == 1))
                        if g == 0:
                            ins = pe.matmul(b[:, 0:nk], sel[:, s, :], fx[:, 3, 0:nk], start=False, stop=True)
                        done(ins)
                    if 0 <= s - 2 < HEADS:
                        h = s - 2
                        b = fill(("PT", t, g, h))
                        pe.wait_ge(s_prob, n0 + h + 1)
                        for m in range(t + 1):
                            ins = pe.transpose(b[:, m * P:(m + 1) * P], score[:, h % NS, m * P:(m + 1) * P], ident[:])
                        done(ins)
                    if 0 <= s - 3 < HEADS:
                        h = s - 3
                        key = ("y", t, g, h // 2)
                        b = fill(key) if h % 2 == 0 else bank(key)
                        await_read(pe, ("PT", t, g, h))
                        at = HD * (h % 2)
                        for m in range(t + 1):
                            ins = pe.matmul(b[at:at + HD, 0:P], v_sb[:, m, g, h * HD:(h + 1) * HD], pT[:, h % 2, m, :],
                                            start=(m == 0), stop=(m == t))
                        if h % 2 == 1:
                            done(ins)
                    if t == 0:
                        between(g * STEPS + s)

            def late_chunk(t, key, width):
                no = t * len(late) + late_no[key]
                pe.wait_ge(s_late[no % NL], 16 * (no // NL + 1))
                return late_ring[:, no % NL, :].rearrange("p (k n) -> p k n", n=width)

            def up(t):
                for p_ in range(4):
                    for g in range(2):
                        if p_ == 3:
                            await_read(pe, ("y", t, g, p_))
                for c_ in range(2):
                    for g in range(2):
                        w = late_chunk(t, ("up", c_, g), 512)
                        b = fill(("up", t, c_, g))
                        for k in range(4):
                            ins = pe.matmul(b[:], yT[:, g, k, :], w[:, k, :], start=(k == 0), stop=(k == 3))
                        done(ins)
                for h in range(2):
                    pe.wait_ge(s_xn, TILES + 3 * t + h + 1)
                    turn(("mixT", t, h), [wide[:, (4 * h + j) * P:(4 * h + j + 1) * P] for j in range(4)])

            def out_part(t):
                for h in range(2):
                    await_read(pe, ("mixT", t, h))
                for q in range(4):
                    w = late_chunk(t, ("out", q), 256)
                    b = fill(("o", t, q))
                    for k in range(KD):
                        ins = pe.matmul(b[:, 0:256], tT[:, k, :], w[:, k, :], start=(k == 0), stop=(k == KD - 1))
                    done(ins)
                pe.wait_ge(s_xn, TILES + 3 * t + 3)
                for h in range(2):
                    turn(("h2T", t, h), [h2[:, t, (4 * h + j) * P:(4 * h + j + 1) * P] for j in range(4)])

            def scores(t, part):
                if part == 0:
                    for h in range(2):
                        await_read(pe, ("h2T", t, h))
                for n in range(2 * part, 2 * part + 2):
                    for m in (2 * n, 2 * n + 1):
                        w = late_chunk(t, ("peer", m), 256)
                        b = fill(("qp", t, m))
                        for j in range(2):
                            for k in range(KD):
                                ins = pe.matmul(b[:, j * P:(j + 1) * P], w[:, k, j * P:(j + 1) * P], tT[:, k, :],
                                                start=(k == 0), stop=(k == KD - 1))
                        done(ins)
                    b = fill(("sc", t, n))
                    for m in (2 * n, 2 * n + 1):
                        await_read(pe, ("qp", t, m))
                        for j in range(2):
                            l = 2 * m + j
                            ins = pe.matmul(b[:, (l % 4) * P:(l % 4 + 1) * P], qp[:, m % 2, j, :], skT[:, l, :],
                                            start=True, stop=True)
                    done(ins)

            after = {1: lambda: attention(1, 0), 2: lambda: attention(1, 1), 3: lambda: up(1),
                     4: lambda: out_part(1), 5: lambda: scores(1, 0), 6: lambda: scores(1, 1)}

            def add_rows(i, first, last):
                for k in range(TOPK):
                    pe.wait_ge(s_diag, i * TOPK + (k + 1))
                    pe.wait_ge(s_v[k % NV], i * (16 * (TOPK // NV)) + 16 * (k // NV + 1))
                    for h in range(2):
                        cut = slice(h * HALF, (h + 1) * HALF)
                        ins = pe.matmul(ps_y[:, cut], diag[:, k % ND, :], vbuf[:, k % NV, cut],
                                        start=(first and k == 0), stop=(last and k == TOPK - 1))
                    ins.then_inc(s_vfree, 1)

            attention(0, 0)
            attention(0, 1)
            finish_setup()
            up(0)
            out_part(0)
            scores(0, 0)
            scores(0, 1)
            for i in range(1, HEADS + 1):
                add_rows(i - 1, i == 1, i == HEADS)
                if i in after:
                    after[i]()
            pe.wait_ge(s_ytaken, 1)
            add_rows(HEADS, True, False)
            with pe.Fori(HEADS + 1, NG - 1) as i:
                add_rows(i, False, False)
            add_rows(NG - 1, False, True)


_INS = ["x", "c", "w_ada", "b_ada", "norm1_g", "w_in", "b_fgate", "fox_q_g", "fox_k_g", "moba_q_g", "moba_k_g",
        "w_up_fox", "w_up_moba", "w_out", "norm2_g", "w_peer_q", "peer_sub_keys", "peer_u", "peer_v"]


def kernel(**inputs):
    import numpy as np
    import concourse.bacc as bacc
    from concourse.bass_utils import run_bass_kernel_spmd

    nc = bacc.Bacc("TRN2", target_bir_lowering=False, num_devices=1)
    arrays, args = {}, []
    for name in _INS:
        a = np.ascontiguousarray(inputs[name])
        arrays[f"in_{name}"] = a
        args.append(nc.dram_tensor(f"in_{name}", a.shape, mybir.dt.from_np(a.dtype), kind="ExternalInput").ap())
    out = nc.dram_tensor("out_y", inputs["x"].shape, F32, kind="ExternalOutput").ap()
    block_kernel(nc, *args, out)
    r = run_bass_kernel_spmd(nc, [arrays], core_ids=[0])
    return r.results[0]["out_y"]
```

```python
from contextlib import ExitStack

import concourse.bass as bass
from concourse import mybir

F32 = mybir.dt.float32
F32R = mybir.dt.float32r
U32 = mybir.dt.uint32
I32 = mybir.dt.int32
ALU = mybir.AluOpType
ACT = mybir.ActivationFunctionType
AX_X = mybir.AxisListType.X

P = 128
EPS = 1e-6
NEG = -1e30
HD = 64
HEADS = 8
TOPK = 16
LISTS = 2 * HEADS
WIDE = 4
NARROW = 4
NCAND = WIDE * TOPK + (TOPK - WIDE) * NARROW
NW = 4
NL = 2
NLO = 4
NU = 8
NV = 8
ND = 8
DVE_ROWS = (NV, NV + 2, NV + 4)
NB = 6
NS = 4
QA, VA, KA, QB, KB, VB = range(6)
NZ_QKV = 6
STEPS = HEADS + 3
NZ = 10
ADA = 12
ADA_FIRST = 4
ADA_SPLIT = 6
ADA_LATE = {8: 10, 16: 11}
ADA_LATE_FIRST = min(ADA_LATE.values())

PAIRS = TOPK // 2
GROUPS = [[(0, 1), (1, 1), (2, 2), (4, 2), (6, 2)], [(0, 2), (2, 2), (4, 2), (6, 2)]]
SLOT = {"choice": ((None, None, 7, 11, 15), (59, 63, 67, 71)), "attention": 18, "up": 35, "out": 45, "scores": 55}
ATTENTION_SLOTS = 16


def attention_cuts():
    total = 2 * STEPS
    return [(SLOT["attention"] + n * ATTENTION_SLOTS // total, n // STEPS, n % STEPS) for n in range(total)]


def lay_attention(behind, attention):
    for slot, g, s in attention_cuts():
        behind.setdefault(slot, []).append(lambda g=g, s=s: attention(1, g, range(s, s + 1)))


def psum_plan(tiles):
    items = ["c", "cols"] + [("xT", t, h) for t in range(tiles) for h in range(2)]
    items.append("ada_cols")
    items += [key for key in z_order(tiles) if key[0] != "qkT"]
    for t in range(tiles):
        for g in range(2):
            for s in range(STEPS):
                if s < HEADS:
                    items.append(("S", t, g, s))
                if 0 <= s - 2 < HEADS:
                    items.append(("PT", t, g, s - 2))
                if 0 <= s - 3 < HEADS and (s - 3) % 2 == 1:
                    items.append(("y", t, g, (s - 3) // 2))
                if t == 0 and g * STEPS + s in ADA_LATE:
                    items.append(("ada", ADA_LATE[g * STEPS + s]))
        for c in range(2):
            items += [("up", t, c, g) for g in range(2)]
        items.append(("mixT", t, 0))
        if t == 0:
            items += [("g2", h) for h in range(2)]
        items.append(("mixT", t, 1))
        items += [("o", t, q) for q in range(4)]
        if t == 0:
            items += [("skT", n) for n in range(2)]
        items += [("h2T", t, h) for h in range(2)]
        if t == 0:
            items += [("skT", n) for n in range(2, 4)]
        for m in range(HEADS):
            items += [("qp", t, m)] + [("sc", t, m)] * (len(scored(t, m)) > 0)
    return {key: n for n, key in enumerate(items)}


def scored(t, m):
    if t == 0 and m < 2:
        return [m]
    return [m - 1, m] if m % 2 == 1 else []


def z_order(tiles):
    items = ["f"]
    behind = []
    for c in range(NZ_QKV):
        items += [("z", c, t) for t in range(tiles)]
        items += behind
        behind = [("qkT", c, t) for t in range(tiles)] if c in (QA, KA, QB, KB) else []
        if c == KA:
            items.append("Fcol")
        if c:
            items.append(("ada", ADA_FIRST + c - 1))
    return items + behind + [("ada", ADA_FIRST + NZ_QKV - 1)]


def gate_blocks(u, total):
    return range(u * total // (2 * STEPS), (u + 1) * total // (2 * STEPS))


def block_kernel(nc, x, c, w_ada, b_ada, norm1_g, w_in, b_fgate, fox_q_g, fox_k_g, moba_q_g, moba_k_g,
                 w_up_fox, w_up_moba, w_out, norm2_g, w_peer_q, peer_sub_keys, peer_u, peer_v, out):
    T, D = x.shape[1], x.shape[2]
    TILES = T // P
    KD = D // P
    HALF = D // 2
    NG = TILES * HEADS
    GW = HEADS * HD
    F_AT = 3 * GW
    z_at = [0, 2 * GW, GW] + [F_AT + HEADS + n * GW for n in range(NZ - 3)]
    slopes = [2.0 ** (-8.0 * (h + 1) / HEADS) for h in range(HEADS)]
    plan = psum_plan(TILES)
    assert TILES == 2 and KD == 8 and GW == 512

    chunks = [("ada", n) for n in range(ADA_FIRST)]
    for n in range(ADA - ADA_FIRST):
        chunks += [("z", n), ("ada", ADA_FIRST + n)]
    chunks += [("z", n) for n in range(ADA - ADA_FIRST, NZ)]
    chunks += [("up", 0), ("up", 1), ("out", 0), ("out", 1), ("sk", 0)] + [("peer", n) for n in range(4)]
    chunk_no = {key: n for n, key in enumerate(chunks)}
    late = [("up", c, g) for c in range(2) for g in range(2)]
    late += [("out", n) for n in range(4)] + [("peer", n) for n in range(8)]
    late_no = {key: n for n, key in enumerate(late)}

    with ExitStack() as ctx:
        def sb(name, shape, dt=F32):
            return ctx.enter_context(nc.sbuf_tensor(name, shape, dt))

        def sem(name):
            return ctx.enter_context(nc.semaphore(name))

        ring = sb("ring", [P, NW, KD, 512])
        uv = ring[:].rearrange("p a k n -> p (a k n)").rearrange("p (s d) -> p s d", d=D)
        u_at = (max(n for n, key in enumerate(chunks) if key == ("peer", 0)) % NW) * (8 * 512 // D)

        def u_row(k):
            return uv[:, (u_at + k % NU) % (NU + NV), :]

        def v_row(k):
            return uv[:, (u_at + NU + k % NV) % (NU + NV), :]

        with ExitStack() as first:
            def sb_first(name, shape):
                return first.enter_context(nc.sbuf_tensor(name, shape, F32R))

            hT_hi = sb_first("hT_hi", [P, KD, T])
            hT_lo = sb_first("hT_lo", [P, KD, T])
            w_hi = sb_first("w_hi", [P, KD, 512])
            w_lo = sb_first("w_lo", [P, NLO, 512])
        late_ring = sb("late_ring", [P, NL, 2048])
        sc = sb("sc", [P, LISTS * P])
        tT = sb("tT", [P, KD, P])
        skT = sb("skT", [P, LISTS, P])
        diag = sb("diag", [P, ND, P])
        x_sb = sb("x_sb", [P, TILES, D])
        qkT = sb("qkT", [P, 4, 4, T])
        v_sb = sb("v_sb", [P, TILES, 2, GW])
        gates = sb("gates", [P, TILES, 4, 512])
        hT = gates[:, 0, :, :].rearrange("p a n -> p (a n)").rearrange("p (k t) -> p k t", t=T)
        h2 = gates[:, 0, :, :].rearrange("p a n -> p (a n)").rearrange("p (t d) -> p t d", t=TILES)
        rows = sb("rows", [P, 4, D])
        score = sb("score", [P, NS, T])
        pT = sb("pT", [P, 2, TILES, P])
        tmp = sb("tmp", [P, 2, 512])
        qn = score[:].rearrange("p a n -> p (a n)").rearrange("p (a n) -> p a n", n=512)
        cand = score[:].rearrange("p a n -> p (a n)")[:, 0:HEADS * NCAND].rearrange("p (h n) -> p h n", h=HEADS)
        wide = sb("wide", [P, D])
        yT = sb("yT", [P, 2, 4, P])
        spare = yT[:].rearrange("p a b n -> p (a b n)")
        dist_i = spare[:, 0:T].bitcast(I32)
        pw = spare[:, 0:512].bitcast(U32).rearrange("p (a n) -> p a n", a=4)
        pf = spare[:, 512:1024].rearrange("p (a n) -> p a n", a=4)
        i16f = pT[:].rearrange("p a b n -> p (a b n)")[:, 0:LISTS * TOPK].rearrange("p (l k) -> p l k", k=TOPK)
        qp = sb("qp", [P, 2, 2, P])
        raw = sb("raw", [72, P])
        cols = sb("cols", [P, 72])
        gain = sb("gain", [P, 4])
        group_no = {(t, n): n + t * len(GROUPS[0]) for t in range(TILES) for n in range(len(GROUPS[t]))}
        sums_first = score[:].rearrange("p a n -> p (a n)")[:, 0:D].rearrange("p (a n) -> p a n", a=2)
        sums = wide[:].rearrange("p (a n) -> p a n", a=2)
        silu = sb("silu", [P, KD])
        mod = sb("mod", [P, 16])
        a1 = sb("a1", [P, KD])
        wf = sb("wf", [P, KD, HEADS])
        wf_hi = sb("wf_hi", [P, KD, HEADS], F32R)
        wf_lo = sb("wf_lo", [P, KD, HEADS], F32R)
        bf = sb("bf", [HEADS, 1])
        fx = sb("fx", [HEADS, 4, T])
        sel = sb("sel", [HEADS, HEADS, P])
        fcol = sb("fcol", [P, TILES, HEADS])
        ident = sb("ident", [P, P])
        ones = sb("ones", [P, P])
        mask = sb("mask", [P, T])
        dist = sb("dist", [P, T])
        iota_i = sb("iota_i", [P, TOPK], I32)
        iota_f = sb("iota_f", [P, TOPK])
        ss = sb("ss", [P, TILES * HEADS])
        sq4 = sb("sq4", [P, 4])
        root_of_one = sb("root_of_one", [P, 1])
        nrm = sb("nrm", [P, 4, TILES * HEADS])
        mx = sb("mx", [P, 2, HEADS])
        rsum = sb("rsum", [P, 2, HEADS])
        v16 = sb("v16", [P, LISTS, TOPK])
        i16 = sb("i16", [P, LISTS, TOPK], U32)
        tv = sb("tv", [P, HEADS, TOPK])
        pos = sb("pos", [P, HEADS * TOPK], U32)
        gsum = sb("gsum", [P, 2, HEADS])
        g_sb = sb("g_sb", [P, NG * TOPK])
        eid = sb("eid", [P, NG * TOPK], I32)
        idx = sb("idx", [P, 3, TOPK], I32)
        adot = sb("adot", [P, 2, TOPK])
        gel = sb("gel", [P, TOPK])
        ew = sb("ew", [P, 2, TOPK])

        banks = [ctx.enter_context(nc.psum_tensor(f"bank{b}", [P, 512], F32)) for b in range(NB)]
        ps_y = ctx.enter_context(nc.psum_tensor("ps_y", [P, D], F32))

        s_c = sem("c_loaded")
        s_small = sem("small_loaded")
        s_x = sem("x_loaded")
        s_chunk = [sem(f"chunk_landed{n}") for n in range(NW)]
        s_late = [sem(f"late_landed{n}") for n in range(NL)]
        s_misc = sem("gains_and_forget_weights_loaded")
        s_acc = sem("ada_partials_ready")
        s_summed = sem("ada_partials_summed")
        s_a1 = sem("norm1_factors_ready")
        s_gate = sem("gate_product_ready")
        s_gz = sem("gate_logits_ready")
        s_sigmoid = sem("gate_ready")
        s_const = sem("constants_ready")
        s_pool = sem("pool_step")
        s_dve = sem("dve_step")
        s_item = sem("psum_item_ready")
        s_bank = [sem(f"bank_read{b}") for b in range(NB)]
        s_sig = sem("sigmoid_c_ready")
        s_silu = sem("silu_ready")
        s_sq = sem("squares_ready")
        s_var = sem("variance_ready")
        s_root = sem("root_ready")
        s_xn = sem("row_ready_for_transpose")
        s_fneg = sem("minus_abs_f_ready")
        s_fexp = sem("exp_f_ready")
        s_fone = sem("one_plus_exp_ready")
        s_fln = sem("log_ready")
        s_F = sem("F_ready")
        s_dg = sem("column_diagonal_ready")
        s_sc_max = sem("score_max_ready")
        s_exp = sem("exp_ready")
        s_prob = sem("prob_ready")
        s_h = sem("hT_blocks_ready")
        s_h1 = sem("second_tile_hT_blocks_ready")
        s_h_hi = sem("hT_hi_ready")
        s_h_lo = sem("hT_lo_ready")
        s_wf = sem("forget_weight_part_ready")
        s_turned = sem("q_or_k_turned")
        s_turned_read = sem("q_or_k_in_sbuf")
        s_w_hi = sem("weights_hi_ready")
        s_w_lo = sem("weights_lo_ready")
        s_w_used = sem("weight_block_multiplied")
        s_x1 = sem("x1_ready")
        s_sq4 = sem("x1_squares_summed")
        s_h2 = sem("h2_half_ready")
        s_warm = sem("root_of_one_ready")
        s_g0 = sem("top_scores_shifted")
        s_g1 = sem("top_scores_exp")
        s_eid = sem("expert_ids_ready")
        s_idx = sem("idx_ready")
        s_free = sem("row_slot_seen_free")
        s_u = [sem(f"u_landed{n}") for n in range(NU)]
        s_v = [sem(f"v_landed{n}") for n in range(NV)]
        s_ufree = sem("u_slots_free")
        s_vfree = sem("v_slots_free")
        s_gelu = sem("gelu_ready")
        s_ew = sem("expert_weights_ready")
        s_diag = sem("diag_ready")
        s_half = sem("first_half_of_y_ready")
        s_ytaken = sem("y_read")
        s_yrow = sem("y_row_ready")
        s_stored = sem("stored")

        turned_no = {key: n for n, key in enumerate(("qkT", a, t) for a in (QA, KA, QB, KB) for t in range(TILES))}

        def bank(key):
            if key in turned_no:
                n = turned_no[key] % 2
                return ps_y[:, n * 512:(n + 1) * 512]
            return banks[plan[key] % NB]

        def await_item(eng, key):
            if key in turned_no:
                eng.wait_ge(s_turned, turned_no[key] + 1)
            else:
                eng.wait_ge(s_item, plan[key] + 1)

        def read(ins, key):
            return ins.then_inc(s_turned_read if key in turned_no else s_bank[plan[key] % NB], 1)

        def await_read(eng, key):
            if key in turned_no:
                eng.wait_ge(s_turned_read, turned_no[key] + 1)
            else:
                eng.wait_ge(s_bank[plan[key] % NB], plan[key] // NB + 1)

        def await_chunk_read(eng, n):
            what, m = chunks[n]
            if what == "ada" and m < ADA_FIRST:
                if m < ADA_FIRST - 1:
                    eng.wait_ge(s_summed, m + 1)
                else:
                    await_item(eng, "ada_cols")
            elif what == "ada":
                eng.wait_ge(s_acc, m + 1)
            elif what == "sk":
                await_item(eng, ("skT", 3))
            elif what == "up":
                await_item(eng, ("up", 0, 1, m))
            elif what == "out":
                await_item(eng, ("o", 0, 2 * m + 1))
            elif what == "peer":
                await_item(eng, ("qp", 0, 2 * m + 1))
            else:
                eng.wait_ge(s_w_lo, (m + 1) * KD)

        def await_block(eng, n, k):
            if k < KD - 1:
                eng.wait_ge(s_w_used, n * (KD - 1) + k + 1)
            elif n < NZ_QKV:
                await_item(eng, ("z", n, TILES - 1))
            else:
                eng.wait_ge(s_gate, (n - NZ_QKV + 1) * TILES)

        def gates_done(u):
            return [n // KD * TILES + t for n in gate_blocks(u, 4 * KD) if n % KD == KD - 1 for t in range(TILES)]

        def late_user(no):
            what = late[no]
            return {"up": ("up", 1) + what[1:], "out": ("o", 1) + what[1:], "peer": ("qp", 1) + what[1:]}[what[0]]

        block = ctx.enter_context(nc.Block())

        @block.sync
        def _(sp):
            def late_chunk(no):
                if no >= NL:
                    await_item(sp, late_user(no - NL))
                what = late[no]
                dst = late_ring[:, no % NL, :]
                if what[0] == "up":
                    src = (w_up_fox, w_up_moba)[what[2]][0].rearrange("(k p) n -> p k n", p=P)
                    src = src[:, :, what[1] * 512:(what[1] + 1) * 512]
                    dst = dst.rearrange("p (k n) -> p k n", n=512)
                else:
                    src = (w_out if what[0] == "out" else w_peer_q)[0].rearrange("(k p) n -> p k n", p=P)
                    src = src[:, :, what[1] * 256:(what[1] + 1) * 256]
                    dst = dst.rearrange("p (k n) -> p k n", n=256)
                sp.dma_start(dst, src).then_inc(s_late[no % NL], 16)

            def chunk(n):
                what, m = chunks[n]
                if n >= NW:
                    await_chunk_read(sp, n - NW)
                dst = ring[:, n % NW, :, :]
                if what == "sk":
                    src = peer_sub_keys[0].rearrange("h q n c -> n (h q) c")
                    dst = dst[:, 0:4, :].rearrange("p k (l c) -> p (k l) c", c=P)
                elif what == "up":
                    src = (w_up_fox, w_up_moba)[m][0].rearrange("(k p) n -> p k n", p=P)
                    dst = dst.rearrange("p (k a) n -> p k (a n)", a=2)
                else:
                    w = {"ada": w_ada, "z": w_in, "out": w_out, "peer": w_peer_q}[what]
                    at = z_at[m] if what == "z" else m * 512
                    src = w[0].rearrange("(k p) n -> p k n", p=P)[:, :, at:at + 512]
                sp.dma_start(dst, src).then_inc(s_chunk[n % NW], 16)

            sp.dma_start(raw[0:KD, :], c.rearrange("a (k p) -> (a k) p", p=P)).then_inc(s_c, 16)
            chunk(0)
            for src, at in ((norm1_g, 8), (norm2_g, 16), (b_ada, 24)):
                sp.dma_start(raw[at:at + src.shape[1] // P, :], src.rearrange("a (k p) -> (a k) p", p=P)) \
                  .then_inc(s_small, 16)
            sp.dma_start(x_sb[:], x[0].rearrange("(t p) d -> p t d", p=P)).then_inc(s_x, 16)
            for n in range(1, len(chunks)):
                chunk(n)
            await_block(sp, NZ - 1, KD - 1)
            for no in range(len(late)):
                late_chunk(no)
            for t in range(TILES):
                for h in range(2):
                    cut = slice(h * HALF, (h + 1) * HALF)
                    sp.wait_ge(s_yrow, 2 * t + h + 1)
                    sp.dma_start(out[0, t * P:(t + 1) * P, cut], wide[:, cut]).then_inc(s_stored, 16)
            sp.wait_ge(s_stored, 32 * TILES)

        @block.gpsimd
        def _(pool):
            pool.memset(ones[:], 1.0).then_inc(s_pool, 1)
            pool.memset(ident[:], 0.0).then_inc(s_pool, 1)
            pool.memset(mask[:], 0.0).then_inc(s_pool, 1)
            pool.memset(sel[:], 0.0).then_inc(s_pool, 1)
            pool.iota(dist_i, pattern=[[-1, T]], base=P, channel_multiplier=1).then_inc(s_pool, 1)
            pool.iota(iota_i[:], pattern=[[1, TOPK]], base=0, channel_multiplier=0).then_inc(s_pool, 1)
            pool.wait_ge(s_pool, 6)
            pool.affine_select(out=ident[:], in_=ident[:], compare_op=ALU.not_equal, fill=1.0, base=0,
                               pattern=[[-1, P]], channel_multiplier=1).then_inc(s_const, 1)
            pool.affine_select(out=mask[:], in_=mask[:], compare_op=ALU.is_ge, fill=NEG, base=P,
                               pattern=[[-1, T]], channel_multiplier=1).then_inc(s_const, 1)
            pool.affine_select(out=sel[:], in_=sel[:], compare_op=ALU.not_equal, fill=1.0, base=0,
                               pattern=[[-1, HEADS], [0, P]], channel_multiplier=1).then_inc(s_const, 1)
            pool.tensor_copy(dist[:], dist_i).then_inc(s_pool, 1)
            pool.tensor_copy(iota_f[:], iota_i[:]).then_inc(s_const, 1)
            pool.wait_ge(s_pool, 7)
            pool.affine_select(out=dist[:], in_=dist[:], compare_op=ALU.is_ge, fill=-NEG, base=P,
                               pattern=[[-1, T]], channel_multiplier=1).then_inc(s_const, 1)

            pool.wait_ge(s_misc, 10 * 16)
            pool.tensor_copy(wf_hi[:], wf[:]).then_inc(s_wf, 1)
            pool.wait_ge(s_wf, 1)
            pool.tensor_tensor(wf_lo[:], wf[:], wf_hi[:].bitcast(F32), ALU.subtract).then_inc(s_wf, 1)
            for n in range(NZ):
                no = chunk_no["z", n]
                for k in range(KD):
                    w = ring[:, no % NW, k, :]
                    pool.wait_ge(s_w_hi, n * KD + k + 1)
                    j = n * KD + k
                    if j >= NLO:
                        await_block(pool, (j - NLO) // KD, (j - NLO) % KD)
                    pool.tensor_tensor(w_lo[:, j % NLO, :], w, w_hi[:, k, :].bitcast(F32),
                                       ALU.subtract).then_inc(s_w_lo, 1)

            pool.sem_inc(s_ufree, NU)
            pool.sem_inc(s_vfree, NV)

            def take(i, r):
                pool.wait_ge(s_eid, i + 1)
                pool.sem_inc(s_free, 1)
                pool.tensor_copy(idx[:, r, :], eid[:, bass.ds(i * TOPK, TOPK)]).then_inc(s_idx, 1)
                pool.wait_ge(s_idx, i + 1)
                pool.sem_inc(s_free, 1)

            def fetch_u(i, k, r):
                pool.wait_ge(s_ufree, i * TOPK + k + 1)
                pool.sem_inc(s_free, 1)
                pool.indirect_dma_start(
                    u_row(k), None, peer_u[0],
                    bass.IndirectOffsetOnAxis(ap=idx[:, r, k:k + 1], axis=0)).then_inc(s_u[k % NU], 16)

            def fetch_v(i, k, r):
                pool.wait_ge(s_vfree, i * TOPK + k + 1)
                pool.sem_inc(s_free, 1)
                pool.indirect_dma_start(
                    v_row(k), None, peer_v[0],
                    bass.IndirectOffsetOnAxis(ap=idx[:, r, k:k + 1], axis=0)).then_inc(s_v[k % NV], 16)

            take(0, 0)
            for k in range(TOPK):
                if k < NU and k % 4 == 0:
                    await_chunk_read(pool, chunk_no["peer", k // 4])
                fetch_u(0, k, 0)
            await_chunk_read(pool, chunk_no["peer", 3])
            with pool.Fori(0, (NG - 1) // 3) as n:
                for j in range(3):
                    i = n * 3 + (1 + j)
                    take(i, (j + 1) % 3)
                    for k in range(TOPK):
                        fetch_u(i, k, (j + 1) % 3)
                        fetch_v(i - 1, k, j)
            for k in range(TOPK):
                fetch_v(NG - 1, k, 0)

        @block.vector
        def _(dve):
            steps = [0]

            def link(ins):
                steps[0] += 1
                ins.then_inc(s_dve, 1)
                dve.wait_ge(s_dve, steps[0])

            roots = [0]
            squares = [0]

            def inverse_root(n, count):
                v, r, q, m = (nrm[:, j, 0:count] for j in range(4))
                roots[0] += 1
                dve.tensor_scalar(v, ss[:, 0:count], 1.0 / n, EPS, ALU.mult, ALU.add).then_inc(s_var, 1)
                dve.wait_ge(s_root, roots[0])
                link(dve.reciprocal(r, q))
                link(dve.tensor_tensor(m, r, r, ALU.mult))
                link(dve.tensor_tensor(m, m, v, ALU.mult))
                link(dve.tensor_scalar(m, m, -0.5, 1.5, ALU.mult, ALU.add))
                link(dve.tensor_tensor(v, r, m, ALU.mult))

            def partials(first, last):
                for j in range(first, last):
                    n, k = j // KD, j % KD
                    acc = sums[:, n % 2, :]
                    no = chunk_no["ada", n]
                    w = ring[:, no % NW, k, :]
                    if k == 0:
                        dve.wait_ge(s_chunk[no % NW], 16 * (no // NW + 1))
                        if n >= ADA_FIRST + 2:
                            await_item(dve, ("ada", n - 2))
                        link(dve.tensor_scalar(acc, w, silu[:, 0:1], None, ALU.mult))
                        continue
                    link(dve.scalar_tensor_tensor(out=acc, in0=w, scalar=silu[:, k:k + 1], in1=acc,
                                                  op0=ALU.mult, op1=ALU.add))
                    if k == KD - 1:
                        for m in range(4):
                            part = acc[:, m * P:(m + 1) * P]
                            at = 24 + 4 * n + m
                            ins = dve.scalar_tensor_tensor(out=part, in0=ident[:], scalar=cols[:, at:at + 1],
                                                           in1=part, op0=ALU.mult, op1=ALU.add)
                        ins.then_inc(s_acc, 1)

            def partials_first(n):
                acc = sums_first[:, n % 2, :]
                dve.wait_ge(s_chunk[n % NW], 16)
                if n >= 2:
                    dve.wait_ge(s_summed, n - 1)
                ins = dve.tensor_scalar(acc, ring[:, n, 0, :], silu[:, 0:1], None, ALU.mult)
                for k in range(1, ADA_SPLIT):
                    link(ins)
                    ins = dve.scalar_tensor_tensor(out=acc, in0=ring[:, n, k, :], scalar=silu[:, k:k + 1],
                                                   in1=acc, op0=ALU.mult, op1=ALU.add)
                ins.then_inc(s_acc, 1)

            await_item(dve, "c")
            read(dve.tensor_copy(cols[:, 0:KD], bank("c")[:, 0:KD]), "c")
            await_read(dve, "c")
            dve.wait_ge(s_sig, 1)
            dve.tensor_tensor(silu[:], silu[:], cols[:, 0:KD], ALU.mult).then_inc(s_silu, 1)
            dve.wait_ge(s_silu, 1)
            partials_first(0)
            await_item(dve, "cols")
            read(dve.tensor_copy(cols[:, KD:72], bank("cols")[:, KD:72]), "cols")
            await_read(dve, "cols")
            for t in range(TILES):
                dve.wait_ge(s_sq, t + 1)
                inverse_root(D, 1)
                if t:
                    await_item(dve, ("xT", t - 1, 1))
                dve.tensor_scalar(wide[:], x_sb[:, t, :], nrm[:, 0, 0:1], None, ALU.mult).then_inc(s_xn, 1)
                dve.wait_ge(s_xn, t + 1)
            for n in range(1, ADA_FIRST):
                partials_first(n)
            await_item(dve, "ada_cols")
            b = bank("ada_cols")
            link(dve.tensor_tensor(mod[:], b[:, 0:4 * ADA_FIRST], cols[:, 24:24 + 4 * ADA_FIRST], ALU.add))
            read(dve.tensor_tensor(mod[:], mod[:], b[:, 4 * ADA_FIRST:8 * ADA_FIRST], ALU.add), "ada_cols")
            await_read(dve, "ada_cols")
            dve.scalar_tensor_tensor(out=a1[:], in0=mod[:, 8:16], scalar=1.0, in1=cols[:, 8:16],
                                     op0=ALU.add, op1=ALU.mult).then_inc(s_a1, 1)
            dve.wait_ge(s_a1, 1)
            for n in range(KD // 2):
                for k in (2 * n, 2 * n + 1):
                    key = ("xT", 0, k // 4)
                    ins = dve.tensor_scalar(hT[:, k, 0:P], bank(key)[:, (k % 4) * P:(k % 4 + 1) * P],
                                            a1[:, k:k + 1], mod[:, k:k + 1], ALU.mult, ALU.add)
                    if k % 4 == 3:
                        read(ins, key)
                    else:
                        ins.then_inc(s_h, 1)
            for n in range(KD // 2):
                cut = slice(2 * n, 2 * n + 2)
                dve.wait_ge(s_h_hi, n + 1)
                dve.tensor_tensor(hT_lo[:, cut, :], hT[:, cut, :], hT_hi[:, cut, :].bitcast(F32),
                                  ALU.subtract).then_inc(s_h_lo, 1)
            dve.wait_ge(s_misc, 10 * 16)
            for n in (0, 2):
                link(dve.tensor_scalar(gain[:, n:n + 1], gain[:, n:n + 1], HD ** -0.5, None, ALU.mult))

            xs, a, b, neg = (fx[:, n, :] for n in range(4))

            def forget_logits():
                await_item(dve, "f")
                read(dve.tensor_scalar(xs, bank("f")[0:HEADS, 0:T], bf[:, 0:1], None, ALU.add), "f")
                await_read(dve, "f")
                link(dve.scalar_tensor_tensor(out=a, in0=xs, scalar=-1.0, in1=xs, op0=ALU.mult, op1=ALU.min))
                dve.tensor_scalar(xs, xs, 0.0, None, ALU.min).then_inc(s_fneg, 1)
                dve.wait_ge(s_fneg, 1)

            def forget_gates():
                dve.wait_ge(s_fexp, 1)
                dve.tensor_scalar(b, b, 1.0, None, ALU.add).then_inc(s_fone, 1)
                dve.wait_ge(s_fln, 1)
                link(dve.tensor_tensor(xs, xs, a, ALU.subtract))
                link(dve.memset(b, 1.0))
                link(dve.tensor_tensor_scan(a, b, xs, 0.0, ALU.mult, ALU.add))
                dve.tensor_scalar(neg, a, -1.0, None, ALU.mult).then_inc(s_F, 1)

            partials(ADA_FIRST * KD, (ADA_FIRST + 1) * KD)
            forget_logits()
            norms = 0
            for c_ in range(NZ_QKV):
                if c_:
                    n = ADA_FIRST + c_
                    partials(n * KD, (n + 1) * KD)
                if c_ == QB:
                    await_item(dve, "Fcol")
                    dve.tensor_copy(fcol[:].rearrange("p t h -> p (t h)"),
                                    bank("Fcol")[:, 0:TILES * HEADS]).then_inc(s_bank[plan["Fcol"] % NB], 1)
                if c_ not in (QA, KA, QB, KB):
                    continue
                for t in range(TILES):
                    dve.wait_ge(s_sq, TILES + norms + t + 1)
                    link(dve.tensor_reduce(ss[:, t * HEADS:(t + 1) * HEADS],
                                           tmp[:, t, :].rearrange("p (h d) -> p h d", d=HD), AX_X, ALU.add))
                inverse_root(HD, TILES * HEADS)
                for t in range(TILES):
                    key = ("z", c_, t)
                    if norms >= 2:
                        pc, pt = [(a, b) for a in (QA, KA, QB, KB) for b in range(TILES)][norms - 2]
                        await_item(dve, ("qkT", pc, pt))
                    ins = dve.tensor_tensor(
                        qn[:, norms % 2, :].rearrange("p (h d) -> p h d", d=HD),
                        bank(key)[:].rearrange("p (h d) -> p h d", d=HD),
                        nrm[:, 0, t * HEADS:(t + 1) * HEADS].unsqueeze(2).to_broadcast([P, HEADS, HD]), ALU.mult)
                    read(ins, key)
                    norms += 1
                if c_ == QA:
                    forget_gates()
            def between(u):
                first = ADA_LATE_FIRST * KD + u
                partials(first, min(first + 1, ADA * KD))

            def norm2_scale():
                for n in (8, 9):
                    await_read(dve, ("ada", n))
                for h in range(2):
                    key = ("g2", h)
                    await_item(dve, key)
                    cut = slice(h * HALF, (h + 1) * HALF)
                    read(dve.scalar_tensor_tensor(out=rows[:, 1, cut], in0=rows[:, 1, cut], scalar=1.0,
                                                  in1=bank(key)[:], op0=ALU.add, op1=ALU.mult), key)
                    await_read(dve, key)

            def attention(t, g, steps_=range(STEPS)):
                nk = (t + 1) * P
                n0 = (t * 2 + g) * HEADS
                par = g
                for s in steps_:
                    if s < HEADS:
                        key = ("S", t, g, s)
                        sl = score[:, s % NS, 0:nk]
                        await_item(dve, key)
                        if n0 + s >= NS:
                            o = n0 + s - NS
                            await_item(dve, ("PT", o // (2 * HEADS), o // HEADS % 2, o % HEADS))
                        if g == 0:
                            ins = dve.scalar_tensor_tensor(out=sl, in0=bank(key)[:, 0:nk], scalar=fcol[:, t, s:s + 1],
                                                           in1=mask[:, T - nk:T], op0=ALU.add, op1=ALU.add)
                        else:
                            ins = dve.scalar_tensor_tensor(out=sl, in0=dist[:, T - nk:T], scalar=-slopes[s],
                                                           in1=bank(key)[:, 0:nk], op0=ALU.mult, op1=ALU.add)
                        read(ins, key)
                        await_read(dve, key)
                        link(dve.tensor_reduce(mx[:, par, s:s + 1], sl, AX_X, ALU.max))
                        dve.tensor_scalar(mx[:, par, s:s + 1], mx[:, par, s:s + 1], -1.0, None,
                                          ALU.mult).then_inc(s_sc_max, 1)
                    if 1 <= s <= HEADS:
                        o = s - 1
                        dve.wait_ge(s_exp, n0 + o + 1)
                        link(dve.reciprocal(rsum[:, par, o:o + 1], rsum[:, par, o:o + 1]))
                        po = score[:, o % NS, 0:nk]
                        dve.tensor_scalar(po, po, rsum[:, par, o:o + 1], None, ALU.mult).then_inc(s_prob, 1)
                    if t == 0:
                        between(g * STEPS + s)

            def up(t, c_, g):
                key = ("up", t, c_, g)
                await_item(dve, key)
                dve.wait_ge(s_sigmoid, 4 * t + 2 * c_ + g + 1)
                read(dve.tensor_tensor(tmp[:, g, :], gates[:, t, 2 * g + c_, :], bank(key)[:], ALU.mult), key)
                await_read(dve, key)
                if g == 1:
                    dve.tensor_tensor(wide[:, c_ * 512:(c_ + 1) * 512], tmp[:, 0, :], tmp[:, 1, :],
                                      ALU.add).then_inc(s_xn, 1)
                    dve.wait_ge(s_xn, TILES + t * 2 + c_ + 1)

            def out_part(t, q):
                key = ("o", t, q)
                cut = slice(q * 256, (q + 1) * 256)
                await_item(dve, key)
                read(dve.tensor_tensor(tmp[:, q % 2, 0:256], bank(key)[:, 0:256], rows[:, 0, cut], ALU.mult), key)
                await_read(dve, key)
                dve.tensor_tensor(x_sb[:, t, cut], x_sb[:, t, cut], tmp[:, q % 2, 0:256],
                                  ALU.add).then_inc(s_x1, 1)
                dve.wait_ge(s_x1, t * 4 + q + 1)
                dve.tensor_tensor_reduce(tmp[:, q % 2, 256:512], x_sb[:, t, cut], x_sb[:, t, cut], 1.0, 0.0,
                                         ALU.mult, ALU.add, sq4[:, q:q + 1]).then_inc(s_sq4, 1)
                link(dve.tensor_tensor(h2[:, t, cut], x_sb[:, t, cut], rows[:, 1, cut], ALU.mult))
                dve.wait_ge(s_sq4, t * 4 + q + 1)

            def norm2(t):
                link(dve.tensor_reduce(ss[:, 0:1], sq4[:], AX_X, ALU.add))
                inverse_root(D, 1)
                for h in range(2):
                    cut = slice(h * HALF, (h + 1) * HALF)
                    dve.scalar_tensor_tensor(out=h2[:, t, cut], in0=h2[:, t, cut], scalar=nrm[:, 0, 0:1],
                                             in1=rows[:, 2, cut], op0=ALU.mult, op1=ALU.add).then_inc(s_h2, 1)
                dve.wait_ge(s_h2, 2 * t + 2)

            def top16(values, indices, scores, n):
                for half in range(2):
                    cut = slice(8 * half, 8 * half + 8)
                    for l in range(n):
                        ins = dve.max(values(l)[:, cut], scores(l))
                    link(ins)
                    for l in range(n):
                        ins = dve.max_index(indices(l)[:, cut], values(l)[:, cut], scores(l))
                    link(ins)
                    if half == 0:
                        for l in range(n):
                            ins = dve.match_replace(scores(l), values(l)[:, cut], scores(l), -3.0e38)
                        link(ins)

            def choose_keys(t, n):
                h, nh = GROUPS[t][n]
                await_read(dve, ("sc", t, h + nh - 1))
                top16(lambda l: v16[:, 2 * h + l, :], lambda l: i16[:, 2 * h + l, :],
                      lambda l: sc[:, (2 * h + l) * P:(2 * h + l + 1) * P], 2 * nh)

            def choose_pairs(t, n):
                h, nh = GROUPS[t][n]
                lists = slice(2 * h, 2 * (h + nh))
                s1 = v16[:, lists, :].rearrange("p (h q) k -> p h q k", q=2)
                link(dve.tensor_copy(i16f[:, lists, :], i16[:, lists, :]))
                cd = cand[:, h:h + nh, :]
                c1 = cd[:, :, 0:WIDE * TOPK].rearrange("p h (a b) -> p h a b", b=TOPK)
                c2 = cd[:, :, WIDE * TOPK:NCAND].rearrange("p h (a b) -> p h a b", b=NARROW)
                link(dve.tensor_tensor(c1, s1[:, :, 0, 0:WIDE].unsqueeze(3).to_broadcast([P, nh, WIDE, TOPK]),
                                       s1[:, :, 1, :].unsqueeze(2).to_broadcast([P, nh, WIDE, TOPK]), ALU.add))
                link(dve.tensor_tensor(
                    c2, s1[:, :, 0, WIDE:TOPK].unsqueeze(3).to_broadcast([P, nh, TOPK - WIDE, NARROW]),
                    s1[:, :, 1, 0:NARROW].unsqueeze(2).to_broadcast([P, nh, TOPK - WIDE, NARROW]), ALU.add))
                p3 = pos[:, 0:nh * TOPK].rearrange("p (h k) -> p h k", k=TOPK)
                top16(lambda l: tv[:, l, :], lambda l: p3[:, l, :], lambda l: cd[:, l, :], nh)

            def choose_experts(t, n):
                h, nh = GROUPS[t][n]
                nk = nh * TOPK
                lists = slice(2 * h, 2 * (h + nh))
                tp = tv[:, 0:nh, :]
                at = t * P + h * TOPK
                gt = g_sb[:, at:at + nk].rearrange("p (h k) -> p h k", k=TOPK)
                dve.tensor_tensor(gt, tp, tp[:, :, 0:1].to_broadcast([P, nh, TOPK]),
                                  ALU.subtract).then_inc(s_g0, 1)
                lo, hi, l2, h2_ = (pw[:, n, 0:nk] for n in range(4))
                af, bf_, m, d = (pf[:, n, 0:nk] for n in range(4))
                ps = pos[:, 0:nk]
                link(dve.tensor_scalar(hi, ps, 4, None, ALU.logical_shift_right))
                link(dve.tensor_scalar(lo, ps, TOPK - 1, None, ALU.bitwise_and))
                link(dve.tensor_scalar(h2_, ps, 2, None, ALU.logical_shift_right))
                link(dve.tensor_scalar(l2, ps, NARROW - 1, None, ALU.bitwise_and))
                link(dve.tensor_scalar(m, ps, float(WIDE * TOPK), None, ALU.is_ge))
                link(dve.scalar_tensor_tensor(out=d, in0=h2_, scalar=float(WIDE - WIDE * TOPK // NARROW), in1=hi,
                                              op0=ALU.add, op1=ALU.subtract))
                link(dve.tensor_tensor(d, d, m, ALU.mult))
                link(dve.tensor_tensor(af, d, hi, ALU.add))
                link(dve.tensor_tensor(d, l2, lo, ALU.subtract))
                link(dve.tensor_tensor(d, d, m, ALU.mult))
                link(dve.tensor_tensor(bf_, d, lo, ALU.add))
                ii = i16f[:, lists, :].rearrange("p (h q) k -> p h q k", q=2)
                place = sc[:, h * TOPK * TOPK:(h * TOPK + nk) * TOPK]
                oh = place.rearrange("p (h k r) -> p h k r", h=nh, k=TOPK)
                oh2 = place.rearrange("p (k r) -> p k r", r=TOPK)
                for rank, q, to in ((af, 0, m), (bf_, 1, d)):
                    link(dve.tensor_tensor(oh2, rank.unsqueeze(2).to_broadcast([P, nk, TOPK]),
                                           iota_f[:].unsqueeze(1).to_broadcast([P, nk, TOPK]), ALU.is_equal))
                    link(dve.tensor_tensor(oh, oh, ii[:, :, q, :].unsqueeze(2).to_broadcast([P, nh, TOPK, TOPK]),
                                           ALU.mult))
                    link(dve.tensor_reduce(to, oh2, AX_X, ALU.add))
                dve.scalar_tensor_tensor(out=eid[:, at:at + nk], in0=m, scalar=float(P), in1=d,
                                         op0=ALU.mult, op1=ALU.add).then_inc(s_eid, nh)
                dve.wait_ge(s_g1, group_no[t, n] + 1)
                link(dve.tensor_reduce(gsum[:, 0, 0:nh], gt, AX_X, ALU.add))
                link(dve.reciprocal(gsum[:, 1, 0:nh], gsum[:, 0, 0:nh]))
                link(dve.tensor_tensor(gt, gt, gsum[:, 1, 0:nh].unsqueeze(2).to_broadcast([P, nh, TOPK]), ALU.mult))

            behind = {}
            lay_attention(behind, attention)
            for n in range(4):
                behind[SLOT["up"] + 2 * n + 2] = [lambda n=n: up(1, n // 2, n % 2)]
                behind[SLOT["out"] + 2 * n + 2] = [lambda n=n: out_part(1, n)]
            behind[SLOT["out"] + 8].append(lambda: norm2(1))
            for t in range(TILES):
                for n in range(0 if t else 2, len(GROUPS[t])):
                    at = SLOT["choice"][t][n]
                    behind.setdefault(at, []).append(lambda t=t, n=n: choose_keys(t, n))
                    behind.setdefault(at + 2, []).append(lambda t=t, n=n: (choose_pairs(t, n), choose_experts(t, n)))

            def run(slot):
                for stage in behind.get(slot, ()):
                    stage()

            def dots(i, par, t, slot=None):
                for k in range(TOPK):
                    dve.wait_ge(s_u[k % NU], i * (16 * (TOPK // NU)) + 16 * (k // NU + 1))
                    dve.tensor_tensor_reduce(u_row(k), u_row(k), h2[:, t, :], 1.0, 0.0,
                                             ALU.mult, ALU.add, adot[:, par, k:k + 1]).then_inc(s_ufree, 1)
                    if slot is not None and k % 2 == 1 and k < TOPK - 1:
                        run(slot + k // 2)
                dve.wait_ge(s_gelu, i + 1)
                dve.tensor_tensor(ew[:, par, :], g_sb[:, bass.ds(i * TOPK, TOPK)], gel[:],
                                  ALU.mult).then_inc(s_ew, 1)
                if slot is not None:
                    run(slot + PAIRS - 1)

            def last_dots():
                i, par = NG - 1, (NG - 1) % 2
                for k in range(TOPK):
                    dve.wait_ge(s_u[k % NU], i * (16 * (TOPK // NU)) + 16 * (k // NU + 1))
                    dve.tensor_tensor_reduce(u_row(k), u_row(k), h2[:, 1, :], 1.0, 0.0,
                                             ALU.mult, ALU.add, adot[:, par, k:k + 1]).then_inc(s_ufree, 1)
                    if k % 4 == 3:
                        four = slice(k - 3, k + 1)
                        dve.wait_ge(s_gelu, i + k // 4 + 1)
                        dve.tensor_tensor(ew[:, par, four], g_sb[:, i * TOPK + k - 3:i * TOPK + k + 1],
                                          gel[:, four], ALU.mult).then_inc(s_ew, 1)

            def last_rows():
                i, par = NG - 1, (NG - 1) % 2
                acc = tmp[:].rearrange("p a n -> p (a n)")
                dve.wait_ge(s_ew, i + 4)
                for k in DVE_ROWS:
                    dve.wait_ge(s_v[k % NV], i * (16 * (TOPK // NV)) + 16 * (k // NV + 1))
                    if k == DVE_ROWS[0]:
                        link(dve.tensor_scalar(acc, v_row(k), ew[:, par, k:k + 1], None, ALU.mult))
                    else:
                        link(dve.scalar_tensor_tensor(out=acc, in0=v_row(k), scalar=ew[:, par, k:k + 1], in1=acc,
                                                      op0=ALU.mult, op1=ALU.add))
                link(dve.tensor_tensor(acc, acc, rows[:, 3, :], ALU.mult))
                link(dve.tensor_tensor(x_sb[:, 1, :], x_sb[:, 1, :], acc, ALU.add))

            def finish(t):
                if t:
                    dve.wait_ge(s_stored, 32 * t)
                for h in range(2):
                    if h == 0:
                        dve.wait_ge(s_half, t + 1)
                    else:
                        rest = t * len(DVE_ROWS)
                        dve.wait_ge(s_vfree, NV + (t + 1) * HEADS * TOPK - rest)
                    cut = slice(h * HALF, (h + 1) * HALF)
                    dve.tensor_tensor(wide[:, cut], ps_y[:, cut], rows[:, 3, cut], ALU.mult).then_inc(s_ytaken, 1)
                    dve.wait_ge(s_ytaken, 2 * t + h + 1)
                    dve.tensor_tensor(wide[:, cut], wide[:, cut], x_sb[:, t, cut], ALU.add).then_inc(s_yrow, 1)

            attention(0, 0)
            attention(0, 1)
            await_item(dve, ("ada", ADA - 1))
            for n in range(4):
                up(0, n // 2, n % 2)
            norm2_scale()
            for n in range(4):
                out_part(0, n)
            norm2(0)
            for n in range(2):
                choose_keys(0, n)
                choose_pairs(0, n)
                choose_experts(0, n)
            for i in range(HEADS + 1):
                dots(i, i % 2, i // HEADS, PAIRS * i)
            finish(0)
            dots(HEADS + 1, 1, 1, PAIRS * (HEADS + 1))
            with dve.Fori(1, HEADS // 2 - 1) as n:
                for j in range(2):
                    dots(n * 2 + (HEADS + j), j, 1)
            dots(NG - 2, 0, 1)
            last_dots()
            last_rows()
            finish(1)

        @block.scalar
        def _(act):
            rooted = [0]

            def root(count):
                rooted[0] += 1
                act.wait_ge(s_var, rooted[0])
                act.activation(nrm[:, 2, 0:count], nrm[:, 0, 0:count], ACT.Sqrt).then_inc(s_root, 1)

            await_read(act, "c")
            act.activation(silu[:], cols[:, 0:KD], ACT.Sigmoid).then_inc(s_sig, 1)
            for n, src in enumerate((fox_q_g, fox_k_g, moba_q_g, moba_k_g)):
                for h in range(2):
                    act.dma_start(gain[h * HD:(h + 1) * HD, n:n + 1], src.rearrange("a d -> d a")) \
                       .then_inc(s_misc, 16)
            act.dma_start(bf[:], b_fgate.rearrange("a h -> h a")).then_inc(s_misc, 16)
            act.dma_start(wf[:], w_in[0].rearrange("(k p) n -> p k n", p=P)[:, :, F_AT:F_AT + HEADS]) \
               .then_inc(s_misc, 16)
            for t in range(TILES):
                if t == 0:
                    act.wait_ge(s_x, 16)
                act.activation(tmp[:].rearrange("p a n -> p (a n)"), x_sb[:, t, :], ACT.Square,
                               accum_out=ss[:, 0:1]).then_inc(s_sq, 1)
                root(1)
            act.wait_ge(s_a1, 1)
            for n in range(KD // 2):
                key = ("xT", 1, n // 2)
                for k in (2 * n, 2 * n + 1):
                    ins = act.activation(hT[:, k, P:2 * P], bank(key)[:, (k % 4) * P:(k % 4 + 1) * P],
                                         ACT.Identity, scale=a1[:, k:k + 1], bias=mod[:, k:k + 1])
                if n % 2 == 1:
                    read(ins, key)
                    await_read(act, key)
                    await_read(act, ("xT", 0, n // 2))
                else:
                    ins.then_inc(s_h1, 1)
                    act.wait_ge(s_h1, n // 2 + 1)
                    act.wait_ge(s_h, 3 * (n // 2) + 2)
                cut = slice(2 * n, 2 * n + 2)
                act.activation(hT_hi[:, cut, :], hT[:, cut, :], ACT.Copy).then_inc(s_h_hi, 1)

            def round_weights(first, last):
                for j in range(first, last):
                    n, k = j // KD, j % KD
                    no = chunk_no["z", n]
                    if k == 0:
                        act.wait_ge(s_chunk[no % NW], 16 * (no // NW + 1))
                    if n:
                        await_block(act, n - 1, k)
                    act.activation(w_hi[:, k, :], ring[:, no % NW, k, :], ACT.Copy).then_inc(s_w_hi, 1)

            round_weights(0, KD)

            def forget_logs():
                act.wait_ge(s_fneg, 1)
                act.activation(fx[:, 2, :], fx[:, 1, :], ACT.Exp).then_inc(s_fexp, 1)
                act.wait_ge(s_fone, 1)
                act.activation(fx[:, 1, :], fx[:, 2, :], ACT.Ln).then_inc(s_fln, 1)

            qk_items = [("z", a, b) for a in (QA, KA, QB, KB) for b in range(TILES)]
            qk = 0
            behind = []

            def qk_out():
                c_, t = behind.pop(0)
                key = ("qkT", c_, t)
                await_item(act, key)
                place = (QA, KA, QB, KB).index(c_)
                ins = act.activation(qkT[:, place, :, t * P:(t + 1) * P],
                                     bank(key)[:].rearrange("p (a n) -> p a n", n=P), ACT.Copy,
                                     scale=gain[:, place:place + 1])
                read(ins, key)

            def row_out(n):
                key = ("ada", n)
                await_item(act, key)
                r, h = (0, 2, 1, 3)[(n - ADA_FIRST) // 2], n % 2
                read(act.activation(rows[:, r, h * HALF:(h + 1) * HALF], bank(key)[:], ACT.Copy), key)

            for c_ in range(NZ_QKV):
                round_weights((c_ + 1) * KD, (c_ + 2) * KD)
                for t in range(TILES):
                    key = ("z", c_, t)
                    await_item(act, key)
                    if c_ in (QA, KA, QB, KB):
                        if qk >= 2:
                            await_read(act, qk_items[qk - 2])
                        act.activation(tmp[:, qk % 2, :], bank(key)[:], ACT.Square).then_inc(s_sq, 1)
                        qk += 1
                        if t == TILES - 1:
                            root(TILES * HEADS)
                        behind.append((c_, t))
                    else:
                        read(act.activation(v_sb[:, t, 0 if c_ == VA else 1, :], bank(key)[:], ACT.Copy), key)
                if c_ == QA:
                    forget_logs()
                while behind and behind[0][0] < c_:
                    qk_out()
                if c_:
                    row_out(ADA_FIRST + c_ - 1)
            while behind:
                qk_out()
            row_out(ADA_FIRST + NZ_QKV - 1)
            def between(u):
                ahead = [KD + n for n in (gate_blocks(u - 1, 4 * KD) if u else ()) if n < 3 * KD]
                if ahead:
                    round_weights(NZ_QKV * KD + ahead[0], NZ_QKV * KD + ahead[-1] + 1)
                if u in ADA_LATE:
                    row_out(ADA_LATE[u])
                for m in gates_done(u):
                    act.wait_ge(s_gate, m + 1)
                    act.activation(gates[:, m % TILES, m // TILES, :], ps_y[:, (m % 2) * 512:(m % 2 + 1) * 512],
                                   ACT.Copy).then_inc(s_gz, 1)

            def sigmoids(t):
                act.wait_ge(s_gz, 4 * TILES)
                for c_ in range(2):
                    for g in range(2):
                        z = gates[:, t, 2 * g + c_, :]
                        act.activation(z, z, ACT.Sigmoid).then_inc(s_sigmoid, 1)

            def norm2_diagonals():
                for k in range(KD):
                    act.activation(diag[:, k, :], ident[:], ACT.Copy, scale=cols[:, 16 + k:17 + k]).then_inc(s_dg, 1)

            def keys_out():
                for n in range(4):
                    key = ("skT", n)
                    await_item(act, key)
                    read(act.activation(skT[:, 4 * n:4 * n + 4, :], bank(key)[:].rearrange("p (a n) -> p a n", n=P),
                                        ACT.Copy), key)

            def attention(t, g, steps_=range(STEPS)):
                nk = (t + 1) * P
                n0 = (t * 2 + g) * HEADS
                for s in steps_:
                    if s < HEADS:
                        act.wait_ge(s_sc_max, n0 + s + 1)
                        sl = score[:, s % NS, 0:nk]
                        act.activation(sl, sl, ACT.Exp, bias=mx[:, g, s:s + 1],
                                       accum_out=rsum[:, g, s:s + 1]).then_inc(s_exp, 1)
                    if 0 <= s - 2 < HEADS:
                        h = s - 2
                        key = ("PT", t, g, h)
                        await_item(act, key)
                        read(act.activation(pT[:, h % 2, 0:t + 1, :],
                                            bank(key)[:, 0:nk].rearrange("p (a n) -> p a n", n=P), ACT.Copy), key)
                    if 0 <= s - 3 < HEADS and (s - 3) % 2 == 1:
                        pair = (s - 3) // 2
                        key = ("y", t, g, pair)
                        await_item(act, key)
                        read(act.activation(yT[:, g, pair, :], bank(key)[:, 0:P], ACT.Copy), key)
                    if t == 0:
                        between(g * STEPS + s)

            def to_tT(t, name, h):
                key = (name, t, h)
                await_item(act, key)
                read(act.activation(tT[:, 4 * h:4 * h + 4, :],
                                    bank(key)[:].rearrange("p (a n) -> p a n", n=P), ACT.Copy), key)

            def norm2_root():
                act.activation(root_of_one[:], ones[:, 0:1], ACT.Sqrt).then_inc(s_warm, 1)
                root(1)

            def queries(t, m):
                key = ("qp", t, m)
                await_item(act, key)
                read(act.activation(qp[:, m % 2, :, :],
                                    bank(key)[:, 0:2 * P].rearrange("p (a n) -> p a n", n=P), ACT.Copy), key)
                if scored(t, m):
                    key = ("sc", t, m)
                    first, width = scored(t, m)[0], 2 * P * len(scored(t, m))
                    await_item(act, key)
                    read(act.activation(sc[:, first * 2 * P:first * 2 * P + width],
                                        bank(key)[:, first % 2 * 2 * P:first % 2 * 2 * P + width], ACT.Copy), key)

            def choice(t, n):
                act.wait_ge(s_g0, group_no[t, n] + 1)
                h, nh = GROUPS[t][n]
                gt = g_sb[:, t * P + h * TOPK:t * P + (h + nh) * TOPK]
                act.activation(gt, gt, ACT.Exp).then_inc(s_g1, 1)

            behind = {SLOT["choice"][0][n] + 2: [lambda n=n: choice(0, n)] for n in range(2, 5)}
            lay_attention(behind, attention)
            behind[SLOT["up"] + 6] = [lambda: to_tT(1, "mixT", 0)]
            behind[SLOT["out"]] = [lambda: to_tT(1, "mixT", 1)]
            behind[SLOT["out"] + 8] = [norm2_root]
            behind[SLOT["scores"]] = [lambda h=h: to_tT(1, "h2T", h) for h in range(2)]
            for m in range(8):
                behind.setdefault(SLOT["scores"] + 2 * m, []).append(lambda m=m: queries(1, m))
            for n in range(4):
                behind.setdefault(SLOT["choice"][1][n] + 2, []).append(lambda n=n: choice(1, n))

            def run(slot):
                for stage in behind.get(slot, ()):
                    stage()

            def gelu(i, par):
                act.wait_ge(s_ufree, NU + (i + 1) * TOPK)
                if not isinstance(i, int) or i:
                    act.wait_ge(s_ew, i)
                act.activation(gel[:], adot[:, par, :], ACT.Gelu_apprx_tanh).then_inc(s_gelu, 1)

            def diagonal(i, par, k):
                act.wait_ge(s_vfree, i * TOPK + (k + 1 - ND + NV))
                act.activation(diag[:, k % ND, :], ident[:], ACT.Copy,
                               scale=ew[:, par, k:k + 1]).then_inc(s_diag, 1)

            def diagonals(i, par, slot=None):
                act.wait_ge(s_ew, i + 1)
                for k in range(TOPK):
                    diagonal(i, par, k)
                    if slot is not None and k % 2 == 1:
                        run(slot + k // 2 - 1)

            attention(0, 0)
            attention(0, 1)
            norm2_diagonals()
            sigmoids(0)
            for h in range(2):
                to_tT(0, "mixT", h)
            sigmoids(1)
            norm2_root()
            for h in range(2):
                to_tT(0, "h2T", h)
            keys_out()
            for m in range(8):
                queries(0, m)
                if m == 2:
                    choice(0, 0)
                elif m == 5:
                    choice(0, 1)
            for i in range(HEADS + 2):
                if i:
                    diagonals(i - 1, (i - 1) % 2, PAIRS * i)
                gelu(i, i % 2)
            with act.Fori(1, HEADS // 2 - 1) as n:
                for j in range(2):
                    i = n * 2 + (HEADS + j)
                    diagonals(i - 1, 1 - j)
                    gelu(i, j)
            diagonals(NG - 3, 1)
            gelu(NG - 2, 0)
            act.wait_ge(s_ew, NG - 1)
            for q in range(4):
                for k in range(4 * q, 4 * q + 4):
                    diagonal(NG - 2, 0, k)
                four = slice(4 * q, 4 * q + 4)
                act.wait_ge(s_ufree, NU + (NG - 1) * TOPK + 4 * q + 4)
                act.activation(gel[:, four], adot[:, 1, four], ACT.Gelu_apprx_tanh).then_inc(s_gelu, 1)
            for k in range(TOPK):
                if k not in DVE_ROWS:
                    act.wait_ge(s_ew, NG + k // 4)
                    diagonal(NG - 1, 1, k)

        @block.tensor
        def _(pe):
            def fill(key):
                n = plan[key]
                if n >= NB:
                    pe.wait_ge(s_bank[n % NB], n // NB)
                return banks[n % NB]

            def done(ins):
                return ins.then_inc(s_item, 1)

            def chunk(key):
                n = chunk_no[key]
                pe.wait_ge(s_chunk[n % NW], 16 * (n // NW + 1))
                return ring[:, n % NW, :, :]

            def turn(key, srcs):
                b = fill(key)
                for j, src in enumerate(srcs):
                    ins = pe.transpose(b[:, j * P:(j + 1) * P], src, ident[:])
                done(ins)

            def ada_row(n):
                pe.wait_ge(s_acc, n + 1)
                done(pe.matmul(fill(("ada", n))[:], ones[:], sums[:, n % 2, :], start=True, stop=True))

            def ada_first(n):
                b = bank("ada_cols")
                w = ring[:, n, :, :]
                pe.wait_ge(s_chunk[n], 16)
                for m in range(4):
                    for k in range(ADA_SPLIT, KD):
                        pe.matmul(b[:, 4 * (ADA_FIRST + n) + m:4 * (ADA_FIRST + n) + m + 1],
                                  w[:, k, m * P:(m + 1) * P], silu[:, k:k + 1], start=(k == ADA_SPLIT), stop=(k == KD - 1))
                pe.wait_ge(s_acc, n + 1)
                for m in range(4):
                    ins = pe.matmul(b[:, 4 * n + m:4 * n + m + 1], sums_first[:, n % 2, m * P:(m + 1) * P],
                                    ones[:, 0:1], start=True, stop=True)
                if n < ADA_FIRST - 1:
                    ins.then_inc(s_summed, 1)
                else:
                    done(ins)

            pe.wait_ge(s_c, 16)
            pe.wait_ge(s_const, 1)
            done(pe.transpose(fill("c")[:, 0:KD], raw[0:KD, :], ident[0:KD, 0:KD]))
            pe.wait_ge(s_small, 3 * 16)
            done(pe.transpose(fill("cols")[:, 0:72], raw[:], ident[0:72, 0:72]))
            pe.wait_ge(s_silu, 1)
            fill("ada_cols")
            ada_first(0)
            for t in range(TILES):
                pe.wait_ge(s_xn, t + 1)
                for h in range(2):
                    turn(("xT", t, h), [wide[:, (4 * h + j) * P:(4 * h + j + 1) * P] for j in range(4)])
            for n in range(1, ADA_FIRST):
                ada_first(n)
            pe.wait_ge(s_misc, 10 * 16)

            def z_block(n, k, places, ready):
                lo = w_lo[:, (n * KD + k) % NLO, :]
                pe.wait_ge(s_w_lo, n * KD + k + 1)
                for t, place in enumerate(places):
                    at = slice(t * P, (t + 1) * P)
                    pe.matmul(place, hT_hi[:, k, at], w_hi[:, k, :], start=(k == 0), stop=False)
                    pe.matmul(place, hT_lo[:, k, at], w_hi[:, k, :], start=False, stop=False)
                    ins = pe.matmul(place, hT_hi[:, k, at], lo, start=False, stop=(k == KD - 1))
                    if k == KD - 1:
                        ins.then_inc(ready, 1)
                if k < KD - 1:
                    ins.then_inc(s_w_used, 1)

            for key in z_order(TILES):
                if key == "f":
                    b = fill(key)
                    pe.wait_ge(s_wf, 2)
                    for k in range(KD):
                        pe.wait_ge(s_h_lo, k // 2 + 1)
                        pe.matmul(b[0:HEADS, 0:T], wf_hi[:, k, :], hT_hi[:, k, :], start=(k == 0), stop=False)
                        pe.matmul(b[0:HEADS, 0:T], wf_hi[:, k, :], hT_lo[:, k, :], start=False, stop=False)
                        ins = pe.matmul(b[0:HEADS, 0:T], wf_lo[:, k, :], hT_hi[:, k, :],
                                        start=False, stop=(k == KD - 1))
                    done(ins)
                elif key == "Fcol":
                    pe.wait_ge(s_F, 1)
                    b = fill(key)
                    for t in range(TILES):
                        ins = pe.transpose(b[:, t * HEADS:(t + 1) * HEADS], fx[:, 1, t * P:(t + 1) * P],
                                           ident[0:HEADS, 0:HEADS])
                    done(ins)
                elif key[0] == "ada":
                    ada_row(key[1])
                elif key[0] == "z":
                    if key[2]:
                        continue
                    places = [fill(("z", key[1], t))[:] for t in range(TILES)]
                    for k in range(KD):
                        z_block(key[1], k, places, s_item)
                else:
                    await_read(pe, ("z",) + key[1:])
                    n = turned_no[key]
                    if n >= 2:
                        pe.wait_ge(s_turned_read, n - 1)
                    for j in range(4):
                        ins = pe.transpose(bank(key)[:, j * P:(j + 1) * P], qn[:, n % 2, j * P:(j + 1) * P], ident[:])
                    ins.then_inc(s_turned, 1)
            def between(u):
                if u in ADA_LATE:
                    ada_row(ADA_LATE[u])
                for n in gate_blocks(u, 4 * KD):
                    m, k = n // KD, n % KD
                    if n == 0:
                        pe.wait_ge(s_turned_read, len(turned_no))
                    elif k == 0:
                        pe.wait_ge(s_gz, m * TILES)
                    z_block(NZ_QKV + m, k, [ps_y[:, t * 512:(t + 1) * 512] for t in range(TILES)], s_gate)

            def norm2_rows():
                for h in range(2):
                    pe.wait_ge(s_dg, 4 * h + 4)
                    b = fill(("g2", h))
                    for j in range(4):
                        ins = pe.matmul(b[:, j * P:(j + 1) * P], ones[:], diag[:, 4 * h + j, :], start=True, stop=True)
                    done(ins)

            def turn_keys(h):
                sk = chunk(("sk", 0))
                for n in (2 * h, 2 * h + 1):
                    turn(("skT", n), [sk[:, n, j * P:(j + 1) * P] for j in range(4)])

            pe.wait_ge(s_const, 5)

            def attention(t, g, steps_=range(STEPS)):
                nk = (t + 1) * P
                n0 = (t * 2 + g) * HEADS
                if t == 0 and 0 in steps_:
                    for u in range(TILES):
                        await_read(pe, ("qkT", (QA, QB)[g], u))
                        await_read(pe, ("qkT", (KA, KB)[g], u))
                        await_read(pe, ("z", (VA, VB)[g], u))
                for s in steps_:
                    if s < HEADS:
                        b = fill(("S", t, g, s))
                        at = HD * (s % 2)
                        q = qkT[at:at + HD, 2 * g, s // 2, t * P:(t + 1) * P]
                        k = qkT[at:at + HD, 2 * g + 1, s // 2, 0:nk]
                        ins = pe.matmul(b[:, 0:nk], q, k, start=True, stop=(g == 1))
                        if g == 0:
                            ins = pe.matmul(b[:, 0:nk], sel[:, s, :], fx[:, 3, 0:nk], start=False, stop=True)
                        done(ins)
                    if 0 <= s - 2 < HEADS:
                        h = s - 2
                        b = fill(("PT", t, g, h))
                        pe.wait_ge(s_prob, n0 + h + 1)
                        for m in range(t + 1):
                            ins = pe.transpose(b[:, m * P:(m + 1) * P], score[:, h % NS, m * P:(m + 1) * P], ident[:])
                        done(ins)
                    if 0 <= s - 3 < HEADS:
                        h = s - 3
                        key = ("y", t, g, h // 2)
                        b = fill(key) if h % 2 == 0 else bank(key)
                        await_read(pe, ("PT", t, g, h))
                        at = HD * (h % 2)
                        for m in range(t + 1):
                            ins = pe.matmul(b[at:at + HD, 0:P], v_sb[:, m, g, h * HD:(h + 1) * HD], pT[:, h % 2, m, :],
                                            start=(m == 0), stop=(m == t))
                        if h % 2 == 1:
                            done(ins)
                    if t == 0:
                        between(g * STEPS + s)

            def late_chunk(t, what, m, g=0):
                if t == 0:
                    w = chunk((what, g if what == "up" else m // 2))
                    if what == "up":
                        return w.rearrange("p (k a) n -> p k (a n)", a=2)[:, :, m * 512:(m + 1) * 512]
                    return w[:, :, (m % 2) * 256:(m % 2 + 1) * 256]
                no = late_no[(what, m, g) if what == "up" else (what, m)]
                pe.wait_ge(s_late[no % NL], 16 * (no // NL + 1))
                return late_ring[:, no % NL, :].rearrange("p (k n) -> p k n", n=512 if what == "up" else 256)

            def turn_wide(t, h):
                pe.wait_ge(s_xn, TILES + 2 * t + h + 1)
                turn(("mixT", t, h), [wide[:, (4 * h + j) * P:(4 * h + j + 1) * P] for j in range(4)])

            def up(t, c_, g):
                await_read(pe, ("y", t, 0, 3))
                await_read(pe, ("y", t, 1, 3))
                w = late_chunk(t, "up", c_, g)
                b = fill(("up", t, c_, g))
                for k in range(4):
                    ins = pe.matmul(b[:], yT[:, g, k, :], w[:, k, :], start=(k == 0), stop=(k == 3))
                done(ins)

            def out_part(t, q):
                w = late_chunk(t, "out", q)
                b = fill(("o", t, q))
                for k in range(KD):
                    if k % 4 == 0:
                        await_read(pe, ("mixT", t, k // 4))
                    ins = pe.matmul(b[:, 0:256], tT[:, k, :], w[:, k, :], start=(k == 0), stop=(k == KD - 1))
                done(ins)

            def turn_h2(t):
                for h in range(2):
                    pe.wait_ge(s_h2, 2 * t + h + 1)
                    turn(("h2T", t, h), [h2[:, t, (4 * h + j) * P:(4 * h + j + 1) * P] for j in range(4)])

            def queries(t, m):
                w = late_chunk(t, "peer", m)
                b = fill(("qp", t, m))
                for j in range(2):
                    for k in range(KD):
                        if k % 4 == 0:
                            await_read(pe, ("h2T", t, k // 4))
                        ins = pe.matmul(b[:, j * P:(j + 1) * P], w[:, k, j * P:(j + 1) * P], tT[:, k, :],
                                        start=(k == 0), stop=(k == KD - 1))
                done(ins)
                if scored(t, m):
                    b = fill(("sc", t, m))
                    for m_ in scored(t, m):
                        await_read(pe, ("qp", t, m_))
                        for j in range(2):
                            l = 2 * m_ + j
                            ins = pe.matmul(b[:, (l % 4) * P:(l % 4 + 1) * P], qp[:, m_ % 2, j, :], skT[:, l, :],
                                            start=True, stop=True)
                    done(ins)

            behind = {}
            lay_attention(behind, attention)
            for n in range(4):
                behind[SLOT["up"] + 2 * n] = [lambda n=n: up(1, n // 2, n % 2)]
            behind[SLOT["up"] + 6].append(lambda: turn_wide(1, 0))
            behind[SLOT["out"]] = [lambda: turn_wide(1, 1)]
            for n in range(4):
                behind.setdefault(SLOT["out"] + 2 * n, []).append(lambda n=n: out_part(1, n))
            behind[SLOT["scores"]] = [lambda: turn_h2(1)]
            for m in range(8):
                behind.setdefault(SLOT["scores"] + 2 * m, []).append(lambda m=m: queries(1, m))

            def add_rows(i, first, last, slot=None):
                ks = [k for k in range(TOPK) if not (isinstance(i, int) and i == NG - 1 and k in DVE_ROWS)]
                for n, k in enumerate(ks):
                    pe.wait_ge(s_diag, i * TOPK + (n + 1))
                    pe.wait_ge(s_v[k % NV], i * (16 * (TOPK // NV)) + 16 * (k // NV + 1))
                    for h in range(2):
                        cut = slice(h * HALF, (h + 1) * HALF)
                        ins = pe.matmul(ps_y[:, cut], diag[:, k % ND, :], v_row(k)[:, cut],
                                        start=(first and k == 0), stop=(last and k == TOPK - 1))
                        if h == 0 and last and k == TOPK - 1:
                            ins.then_inc(s_half, 1)
                    ins.then_inc(s_vfree, 1)
                    if slot is not None and k % 2 == 1:
                        for stage in behind.get(slot + k // 2, ()):
                            stage()

            attention(0, 0)
            attention(0, 1)
            for n in range(4):
                up(0, n // 2, n % 2)
            turn_wide(0, 0)
            norm2_rows()
            turn_wide(0, 1)
            for n in range(4):
                out_part(0, n)
            turn_keys(0)
            turn_h2(0)
            turn_keys(1)
            for m in range(8):
                queries(0, m)
            for i in range(1, HEADS + 1):
                add_rows(i - 1, i == 1, i == HEADS, PAIRS * i)
            pe.wait_ge(s_ytaken, 2)
            add_rows(HEADS, True, False)
            with pe.Fori(HEADS + 1, NG - 1) as i:
                add_rows(i, False, False)
            add_rows(NG - 1, False, True)


_INS = ["x", "c", "w_ada", "b_ada", "norm1_g", "w_in", "b_fgate", "fox_q_g", "fox_k_g", "moba_q_g", "moba_k_g",
        "w_up_fox", "w_up_moba", "w_out", "norm2_g", "w_peer_q", "peer_sub_keys", "peer_u", "peer_v"]


def kernel(**inputs):
    import numpy as np
    import concourse.bacc as bacc
    from concourse.bass_utils import run_bass_kernel_spmd

    nc = bacc.Bacc("TRN2", target_bir_lowering=False, num_devices=1)
    arrays, args = {}, []
    for name in _INS:
        a = np.ascontiguousarray(inputs[name])
        arrays[f"in_{name}"] = a
        args.append(nc.dram_tensor(f"in_{name}", a.shape, mybir.dt.from_np(a.dtype), kind="ExternalInput").ap())
    out = nc.dram_tensor("out_y", inputs["x"].shape, F32, kind="ExternalOutput").ap()
    block_kernel(nc, *args, out)
    r = run_bass_kernel_spmd(nc, [arrays], core_ids=[0])
    return r.results[0]["out_y"]
```
